# Optimizing a Trainium2 kernel written in Bass

```python
import jax, jax.numpy as jnp
from jax import lax
import numpy as np

D_MODEL = 1024
BATCH = 1
SEQ = 256
DEPTH = 1

GRID_W = 64
NA_HEADS = 8
NA_HEAD_DIM = 64
NA_WIN_ROWS_MAX = 8
NA_WIN_COLS = 16
NA_WIDTH = NA_HEADS * NA_HEAD_DIM
MLA_HEADS = 8
MLA_Q_LORA = 384
MLA_KV_LORA = 256
MLA_NOPE = 64
MLA_ROPE = 32
MLA_V = 64
MLA_WIDTH = MLA_HEADS * MLA_V
ROPE_THETA = 100.0
Q_BLOCK = 128
IN_COLS = 3 * NA_WIDTH + MLA_Q_LORA + MLA_KV_LORA + MLA_ROPE + 2 * D_MODEL
N_EXPERTS = 32
TOP_K = 4
D_FF = 1024
SWIGLU_ALPHA = 1.702
SWIGLU_LIMIT = 7.0
MOE_BLOCK = 256
RMS_EPS = 1e-6

kernel_name = 'hybrid_na_mla_moe_block'

def rms_norm(x, g):
    xf = x.astype(jnp.float32)
    y = xf * lax.rsqrt(jnp.mean(xf * xf, axis=-1, keepdims=True) + RMS_EPS)
    return (y * g.astype(jnp.float32)).astype(x.dtype)

def rope_2d(x, rows, cols):
    half = MLA_ROPE // 2
    nf = half // 2
    inv = ROPE_THETA ** (-jnp.arange(nf, dtype=jnp.float32) / nf)

    def rot(xa, pos):
        ang = pos.astype(jnp.float32)[:, None] * inv
        cos, sin = jnp.cos(ang), jnp.sin(ang)
        xa = xa.astype(jnp.float32)
        x1, x2 = xa[..., :nf], xa[..., nf:]
        return jnp.concatenate([x1 * cos - x2 * sin, x1 * sin + x2 * cos], axis=-1)

    out = jnp.concatenate([rot(x[..., :half], rows), rot(x[..., half:], cols)], axis=-1)
    return out.astype(x.dtype)

def neighborhood_attention(q, k, v, rpb):
    B, H, S, Dh = q.shape
    rows = S // GRID_W
    kh = min(NA_WIN_ROWS_MAX, rows)
    kw = NA_WIN_COLS
    r = jnp.arange(rows)
    cidx = jnp.arange(GRID_W)
    row_start = jnp.clip(r - kh // 2, 0, rows - kh)
    col_start = jnp.clip(cidx - kw // 2, 0, GRID_W - kw)
    key_rows = row_start[:, None] + jnp.arange(kh)[None, :]
    qg = q.reshape(B, H, rows, GRID_W, Dh)
    kg = k.reshape(B, H, rows, GRID_W, Dh)[:, :, key_rows]
    vg = v.reshape(B, H, rows, GRID_W, Dh)[:, :, key_rows]
    s = jnp.einsum('bhrqd,bhrjkd->bhrqjk', qg, kg).astype(jnp.float32) * (Dh ** -0.5)
    dr = key_rows - r[:, None] + (NA_WIN_ROWS_MAX - 1)
    dc = jnp.clip(cidx[None, :] - cidx[:, None], -(kw - 1), kw - 1) + (kw - 1)
    bias = rpb.astype(jnp.float32)[:, dr][..., dc]
    s = s + bias.transpose(0, 1, 3, 2, 4)[None]
    col_in = (cidx[None, :] >= col_start[:, None]) & (cidx[None, :] < col_start[:, None] + kw)
    s = jnp.where(col_in[None, None, None, :, None, :], s, -1e30)
    p = jax.nn.softmax(s.reshape(B, H, rows, GRID_W, kh * GRID_W), axis=-1)
    p = p.reshape(B, H, rows, GRID_W, kh, GRID_W).astype(v.dtype)
    o = jnp.einsum('bhrqjk,bhrjkd->bhrqd', p, vg)
    return o.reshape(B, H, S, Dh)

def mla_attention(cq_lat, ckv_lat, k_rope, q_norm_g, kv_norm_g, w_uq, w_ukv, rows, cols):
    B, S, _ = cq_lat.shape
    c_q = rms_norm(cq_lat, q_norm_g)
    q = jnp.einsum('bsr,rhd->bhsd', c_q, w_uq)
    q_nope = q[..., :MLA_NOPE]
    q_rope = rope_2d(q[..., MLA_NOPE:], rows, cols)
    c_kv = rms_norm(ckv_lat, kv_norm_g)
    kv = jnp.einsum('bsr,rhd->bhsd', c_kv, w_ukv)
    k_nope, v = kv[..., :MLA_NOPE], kv[..., MLA_NOPE:]
    k_r = rope_2d(k_rope, rows, cols)
    scale = (MLA_NOPE + MLA_ROPE) ** -0.5
    nb = S // Q_BLOCK
    qn_b = q_nope.reshape(B, MLA_HEADS, nb, Q_BLOCK, MLA_NOPE).transpose(2, 0, 1, 3, 4)
    qr_b = q_rope.reshape(B, MLA_HEADS, nb, Q_BLOCK, MLA_ROPE).transpose(2, 0, 1, 3, 4)

    def block(args):
        qn, qr = args
        s = jnp.einsum('bhqd,bhkd->bhqk', qn, k_nope) + jnp.einsum('bhqd,bkd->bhqk', qr, k_r)
        p = jax.nn.softmax(s.astype(jnp.float32) * scale, axis=-1).astype(v.dtype)
        return jnp.einsum('bhqk,bhkd->bhqd', p, v)

    o = lax.map(block, (qn_b, qr_b))
    o = o.transpose(1, 0, 3, 2, 4).reshape(B, S, MLA_WIDTH)
    return o

def clamped_swiglu(hcat):
    x_glu = jnp.minimum(hcat[..., ::2], SWIGLU_LIMIT)
    x_lin = jnp.clip(hcat[..., 1::2], -SWIGLU_LIMIT, SWIGLU_LIMIT)
    return x_glu * jax.nn.sigmoid(SWIGLU_ALPHA * x_glu) * (x_lin + 1)

def moe_ffn(h, w_router, b_router, w1, b1, w2, b2):
    B, S, D = h.shape
    T = B * S
    xf = h.reshape(T, D)
    logits = (xf @ w_router + b_router).astype(jnp.float32)
    top_vals, top_idx = lax.top_k(logits, TOP_K)
    gates = jax.nn.softmax(top_vals, axis=-1)
    n_items = T * TOP_K
    flat_e = top_idx.reshape(-1)
    flat_tok = jnp.arange(n_items, dtype=jnp.int32) // TOP_K
    flat_g = gates.reshape(-1)
    order = jnp.argsort(flat_e)
    e_sorted = flat_e[order]
    counts = jnp.bincount(flat_e, length=N_EXPERTS)
    padded = ((counts + MOE_BLOCK - 1) // MOE_BLOCK) * MOE_BLOCK
    start = jnp.cumsum(counts) - counts
    pend = jnp.cumsum(padded)
    pstart = pend - padded
    dest = pstart[e_sorted] + (jnp.arange(n_items, dtype=jnp.int32) - start[e_sorted])
    nblk = -(-n_items // MOE_BLOCK) + N_EXPERTS
    cap = nblk * MOE_BLOCK
    buf_tok = jnp.zeros((cap,), jnp.int32).at[dest].set(flat_tok[order])
    buf_g = jnp.zeros((cap,), jnp.float32).at[dest].set(flat_g[order])
    blk_e = jnp.minimum(jnp.searchsorted(pend, jnp.arange(nblk) * MOE_BLOCK, side='right'), N_EXPERTS - 1)
    xb = xf[buf_tok].reshape(nblk, MOE_BLOCK, D)

    def expert_block(args):
        xblk, e = args
        hcat = xblk @ w1[e] + b1[e]
        return clamped_swiglu(hcat) @ w2[e] + b2[e]

    yb = lax.map(expert_block, (xb, blk_e)).reshape(cap, D)
    out = jnp.zeros((T, D), h.dtype).at[buf_tok].add(yb * buf_g[:, None].astype(yb.dtype))
    return out.reshape(B, S, D)

def setup_inputs(seed: int = 0) -> dict:
    key = jax.random.key(seed)
    ks = jax.random.split(key, 24)
    L, D, E = DEPTH, D_MODEL, N_EXPERTS
    nrm = lambda k, shape, s: jax.random.normal(k, shape, jnp.float32) * s
    gain = lambda k: 1.0 + nrm(k, (L, D), 0.02)
    return {
        'x': nrm(ks[0], (BATCH, SEQ, D), 1.0),
        'c': nrm(ks[1], (BATCH, D), 1.0),
        'w_ada': nrm(ks[2], (L, D, 6 * D), D ** -0.5),
        'b_ada': nrm(ks[3], (L, 6 * D), 0.02),
        'g_attn_pre': gain(ks[4]),
        'g_attn_post': gain(ks[5]),
        'w_in': nrm(ks[6], (L, D, IN_COLS), D ** -0.5),
        'b_gate': nrm(ks[7], (L, 2 * D), 0.02),
        'na_rpb': nrm(ks[8], (L, NA_HEADS, 2 * NA_WIN_ROWS_MAX - 1, 2 * NA_WIN_COLS - 1), 0.02),
        'q_norm_g': 1.0 + nrm(ks[9], (L, MLA_Q_LORA), 0.02),
        'kv_norm_g': 1.0 + nrm(ks[10], (L, MLA_KV_LORA), 0.02),
        'w_uq': nrm(ks[11], (L, MLA_Q_LORA, MLA_HEADS, MLA_NOPE + MLA_ROPE), MLA_Q_LORA ** -0.5),
        'w_ukv': nrm(ks[12], (L, MLA_KV_LORA, MLA_HEADS, MLA_NOPE + MLA_V), MLA_KV_LORA ** -0.5),
        'w_na_up': nrm(ks[13], (L, NA_WIDTH, D), NA_WIDTH ** -0.5),
        'w_mla_up': nrm(ks[14], (L, MLA_WIDTH, D), MLA_WIDTH ** -0.5),
        'w_out': nrm(ks[15], (L, D, D), D ** -0.5),
        'g_ffn_pre': gain(ks[16]),
        'g_ffn_post': gain(ks[17]),
        'w_router': nrm(ks[18], (L, D, E), D ** -0.5),
        'b_router': nrm(ks[19], (L, E), 0.01),
        'w1': nrm(ks[20], (L, E, D, 2 * D_FF), D ** -0.5),
        'b1': nrm(ks[21], (L, E, 2 * D_FF), 0.01),
        'w2': nrm(ks[22], (L, E, D_FF, D), D_FF ** -0.5),
        'b2': nrm(ks[23], (L, E, D), 0.01),
    }

def reference(x, c, w_ada, b_ada, g_attn_pre, g_attn_post, w_in, b_gate, na_rpb, q_norm_g, kv_norm_g,
              w_uq, w_ukv, w_na_up, w_mla_up, w_out, g_ffn_pre, g_ffn_post, w_router, b_router,
              w1, b1, w2, b2):
    B, S, D = x.shape
    t = jnp.arange(S, dtype=jnp.int32)
    rows, cols = t // GRID_W, t % GRID_W
    split_at = np.cumsum([3 * NA_WIDTH, MLA_Q_LORA, MLA_KV_LORA, MLA_ROPE, D_MODEL]).tolist()
    sc = jax.nn.silu(c)
    for l in range(DEPTH):
        mod = sc @ w_ada[l] + b_ada[l]
        shift_a, scale_a, gate_a, shift_f, scale_f, gate_f = [m[:, None, :] for m in jnp.split(mod, 6, axis=-1)]
        h = rms_norm(x, g_attn_pre[l]) * (1 + scale_a) + shift_a
        proj = h @ w_in[l]
        na_qkv, cq_lat, ckv_lat, k_rope, g_na, g_mla = jnp.split(proj, split_at, axis=-1)
        na_qkv = na_qkv.reshape(B, S, 3, NA_HEADS, NA_HEAD_DIM).transpose(2, 0, 3, 1, 4)
        o_na = neighborhood_attention(na_qkv[0], na_qkv[1], na_qkv[2], na_rpb[l])
        o_na = o_na.transpose(0, 2, 1, 3).reshape(B, S, NA_WIDTH)
        o_mla = mla_attention(cq_lat, ckv_lat, k_rope, q_norm_g[l], kv_norm_g[l], w_uq[l], w_ukv[l], rows, cols)
        gates = jax.nn.sigmoid(jnp.concatenate([g_na, g_mla], axis=-1) + b_gate[l])
        merged = gates[..., :D_MODEL] * (o_na @ w_na_up[l]) + gates[..., D_MODEL:] * (o_mla @ w_mla_up[l])
        y = merged @ w_out[l]
        x = x + gate_a * rms_norm(y, g_attn_post[l])
        h = rms_norm(x, g_ffn_pre[l]) * (1 + scale_f) + shift_f
        y = moe_ffn(h, w_router[l], b_router[l], w1[l], b1[l], w2[l], b2[l])
        x = x + gate_f * rms_norm(y, g_ffn_post[l])
    return x


_drawn_inputs = setup_inputs


def setup_inputs(seed=0):
    import zlib

    import numpy as np

    out = dict(_drawn_inputs(seed))
    spreads = {}
    factors = {'b_gate': 4.25,
     'na_rpb': 8.0,
     'q_norm_g': 8.0,
     'kv_norm_g': 2.95,
     'g_ffn_post': 6.437,
     'b1': 8.0,
     'b2': 8.0}
    for name, (base, spread) in spreads.items():
        noise = np.random.default_rng([zlib.crc32(name.encode()), seed]).standard_normal(out[name].shape)
        drawn = base * np.exp(spread * noise) if base else spread * noise
        out[name] = __import__('jax').numpy.asarray(drawn.astype(out[name].dtype))
    for name, factor in factors.items():
        out[name] = (out[name] * factor).astype(out[name].dtype)
    return out
```

```python
from contextlib import ExitStack

import concourse.bass as bass
from concourse import mybir

F32 = mybir.dt.float32
F32R = mybir.dt.float32r
I32 = mybir.dt.int32
U32 = mybir.dt.uint32
ALU = mybir.AluOpType
ACT = mybir.ActivationFunctionType
AX = mybir.AxisListType.X

P = 128
TT = 2
D = 1024
KD = D // P
BANK = 512
UNIT = 2048
SLOTS = 8
SPLITS = 3
GRID = 64
NA_H, NA_D, NA_W = 8, 64, 512
RPB_R, RPB_C = 15, 31
M_H, NOPE, ROPE, QK = 8, 64, 32, 96
Q_LORA, KV_LORA = 384, 256
LAT = Q_LORA + KV_LORA + ROPE
NE, TOPK = 32, 4
EPS = 1e-6
HALF = P // 2
ALPHA, LIMIT = 1.702, 7.0
FULL = P

C_ID, C_TRI, C_ONE, C_J, C_JM, C_OFF, C_MASK, C_COS, C_SIN = 0, 128, 256, 384, 512, 640, 768, 832, 864
C_ALL = 896
C_FLIP = 896
C_WIDTH = 1024

K = 1024
A_X, A_MOD, A_GBC, A_H, A_HT, A_QKT, A_V, A_G2, A_G3, A_VM, A_MQK, A_GATE, A_TAB, A_ADA, A_END = (
    0, 8 * K, 24 * K, 32 * K, 40 * K, 48 * K, 56 * K, 60 * K, 72 * K, 80 * K, 84 * K, 100 * K, 116 * K,
    128 * K, 136 * K)


def front_jobs():
    jobs = []

    def job(eng, *key):
        jobs.append((key, eng))

    def mod(v):
        for half in range(2):
            job("act" if v in (0, 3) else "dve", "mod", v, half)

    for i in range(NA_H * 6 * GRID // BANK):
        job("dve", "tab", i)
    mod(0), mod(1)
    for tt in range(TT):
        for q in range(2):
            job("dve" if q else "act", "hT", tt, q)
    for tt in range(TT):
        for part in range(2):
            job("act" if part else "dve", "lat", tt, part)
    for name in "qk":
        for c in range(4):
            job("act", name, c)
    for tt in range(TT):
        job("dve", "v", tt)
    for tt in range(TT):
        job("dve", "cqT", tt)
        job("act", "ckT", tt)
    for tt in range(TT):
        for half in range(2):
            job("dve", "uq", tt, half)
    for tt in range(TT):
        for half in range(2):
            job("act", "ukv", tt, half)
    for tt in range(TT):
        for g in range(2):
            job("dve", "mkT", tt, g)
    for tt in range(TT):
        for g in range(2):
            job("act", "mqT", tt, g)
    job("dve", "s", 0)
    job("dve", "s", 1)
    for n in range(16):
        job("act", "pT", n)
        if n + 2 < 16:
            job("dve", "s", n + 2)
        if n % 4 == 3:
            job("dve", "o", n // 4)
        if n % 4 == 2:
            for tt in range(TT):
                job("dve", "gate", n // 4, tt)
        if n in MOD_AFTER:
            mod(MOD_AFTER[n])
    for a in range(4):
        job("dve" if a % 2 else "act", "oT", a)
    for br in range(2):
        for tt in range(TT):
            for half in range(2):
                job("dve", "up", br, tt, half)
    for tt in range(TT):
        for q in range(2):
            job("dve" if q else "act", "mT", tt, q)
    for tt in range(TT):
        for half in range(2):
            job("act", "y", tt, half)
    for tt in range(TT):
        for q in range(2):
            job("dve" if q else "act", "h2T", tt, q)
    for tt in range(TT):
        job("dve", "lg", tt)
    for tt in range(TT):
        job("dve", "pos", tt)
    job("dve", "cnt")
    for tt in range(TT):
        job("dve", "gT", tt)
    for tt in range(TT):
        for half in range(2):
            job("act", "b2", tt, half)
    return jobs


ADA_LATE = (2, 4, 3, 5)
MOD_AFTER = {4: 2, 8: 4, 12: 3, 15: 5}


def front_units():
    units = [("ada", v, u, "dve") for v in (0, 1) for u in range(4)]
    units += [("lat", u, "pe") for u in range(2)] + [("lat", 2, ("lat", 1, 1))]
    units += [(n, u, ("pe", (n, 3))[u]) for n in "qk" for u in range(2)]
    units += [("v", u, ("pe", ("v", 1))[u]) for u in range(2)]
    units += [("uq", u, ("pe", ("uq", 1, 1))[u]) for u in range(2)] + [("ukv", 0, ("ukv", 1, 1))]
    for n in range(16):
        units.append(("ada", ADA_LATE[n // 4], n % 4, "dve"))
        if n % 4 == 2:
            units += [("gate", n // 4, u, ("pe", ("gate", n // 4, 1))[u]) for u in range(2)]
    units += [("up", br, u, ("pe", ("up", br, 1, 1))[u]) for br in range(2) for u in range(2)]
    units += [("out", u, ("pe", ("y", 1, 1))[u == 3]) for u in range(4)]
    return units


UNITS = 4 + 12 * (NE - 1) + 8
POOL_J = (2, 6, 10)
STEP_ORDER = ["g0", "g1", "g2", "g3", "f0", "f1", "f2", "f3", "w", "c0", "c1", "c2", "c3"]
PRE_FILLS = 8
FILLS = PRE_FILLS + 13 * NE - 8
ACT_DRAINS = PRE_FILLS + 5 * NE - 8
DVE_DRAINS = 8 * NE


def last(e):
    return isinstance(e, int) and e == NE - 1


def no_gather(e):
    return isinstance(e, int) and e >= NE - 2


def unit_no(e, j):
    return 4 + 12 * e + j - (4 if last(e) and j >= 8 else 0)


def split_slot(e, j):
    return unit_no(e, j) % SPLITS if isinstance(e, int) else (4 + j) % SPLITS


def ring_slot(e, b, j, base):
    return (base + unit_no(e, j)) % SLOTS if isinstance(e, int) else (base + 4 + 12 * b + j) % SLOTS


def lo_count(e, j):
    missing = 1 if last(e) and j >= 8 else 0
    if j in POOL_J:
        return True, 1 + 3 * e + sum(q in POOL_J for q in range(j + 1)) - missing
    return False, 3 + 9 * e + sum(q not in POOL_J for q in range(j + 1)) - 3 * missing


def lo_count_of_unit(m):
    if m < 4:
        return (True, 1) if m == 2 else (False, m + 1 - (m > 2))
    e, j = divmod(m - 4, 12)
    if e == NE - 1 and j >= 4:
        j += 4
    return lo_count(e, j)


def fills_before(e):
    return PRE_FILLS + 13 * e - (4 if last(e) else 0)


def fill_no(e, kind):
    return fills_before(e) + STEP_ORDER.index(kind) - (4 if no_gather(e) else 0)


def drains(e, kind):
    q = STEP_ORDER.index(kind)
    if kind[0] in "gw":
        return True, PRE_FILLS + 5 * e - (4 if last(e) else 0) + (q + 1 if kind[0] == "g" else 1 if no_gather(e) else 5)
    return False, 8 * e + (q - 3 if kind[0] == "f" else q - 4)


def bank_of(e, kind, b):
    return fill_no(e, kind) % 2 if isinstance(e, int) else (PRE_FILLS + b + STEP_ORDER.index(kind)) % 2


def two_before(e, kind):
    seq = STEP_ORDER[4:] if no_gather(e) else STEP_ORDER
    q = seq.index(kind)
    if q >= 2:
        return drains(e, seq[q - 2])
    if isinstance(e, int) and e == 0:
        return True, PRE_FILLS - 1 + q
    return drains(e - 1, ["c2", "c3"][q])


def build(nc, x, c, w_ada, b_ada, g_attn_pre, g_attn_post, w_in, b_gate, na_rpb, q_norm_g, kv_norm_g,
          w_uq, w_ukv, w_na_up, w_mla_up, w_out, g_ffn_pre, g_ffn_post, w_router, b_router,
          w1, b1, w2, b2, consts, out, full=FULL, half_cap=HALF):
    units = front_units()
    jobs = front_jobs()
    NF = len(units)
    assert (UNITS % SLOTS, UNITS % SPLITS) == (0, 0)

    table, seen, turn, fills = {}, {"act": 0, "dve": 0}, 0, 0
    bank_last = {}
    for key, eng in jobs:
        seen[eng] += 1
        if key[0] == "o":
            bank = 6 + key[1] % 2
        else:
            bank, turn = turn % 6, turn + 1
        fills += key[0] != "o"
        table[key] = (fills, bank, bank_last.get(bank), eng, seen[eng])
        bank_last[bank] = key
    front_drains = dict(seen)

    with ExitStack() as ctx:
        def tile(name, shape, dt=F32):
            return ctx.enter_context(nc.sbuf_tensor("t_" + name, shape, dt))

        def sem(name):
            return ctx.enter_context(nc.semaphore(name))

        ring = tile("ring", [P, SLOTS, UNIT])
        con = tile("con", [P, C_ALL])
        b1t = tile("b1t", [P, NE, 16])
        ptab = tile("ptab", [P, NE + 2, 10])
        cnt_i = tile("cnt_i", [P, NE], I32)
        ovf_i = tile("ovf_i", [P, 1], I32)
        st = tile("st", [P, 96])
        mx = tile("mx", [P, 2, 2])
        nmx = tile("nmx", [P, 2, 2])
        lsum = tile("lsum", [P, 32])
        linv = tile("linv", [P, 32])
        lo_off = -(-nc.sbuf_base // 64) * 64
        tile("arena", [P, (A_END + 64) // 4])

        def at(name, off, shape, dt=F32):
            return nc.alloc_sbuf_tensor_at("a_" + name, shape, dt, offset=lo_off + off)

        ident, tri, ones = (con[:, o:o + P] for o in (C_ID, C_TRI, C_ONE))
        iota, iota_mod, offdiag = (con[:, o:o + P] for o in (C_J, C_JM, C_OFF))

        xt = at("x", A_X, [P, TT, D])
        modv = at("mod", A_MOD, [P, 4, D])
        MODV = {0: 0, 1: 1, 2: 2, 4: 3, 3: 0, 5: 1}
        gbc = at("gbc", A_GBC, [P, 2, D])
        h = at("h", A_H, [P, TT, D])
        qm = at("qm", A_H, [P, TT, M_H * QK])
        hT = at("hT", A_HT, [P, KD, TT * P])
        qT = at("qT", A_QKT, [P, 4, TT * P])
        kT = at("kT", A_QKT + 4 * K, [P, 4, TT * P])
        ysb = at("ysb", A_QKT, [P, TT, D])
        v_na = at("v_na", A_V, [P, TT, NA_W])
        lat = at("lat", A_G2, [P, TT, LAT])
        cT = at("cT", A_G2 + 5632, [P, 5, TT * P])
        s_sb = at("s_sb", A_G2, [P, 2, 2, 256])
        p_sb = at("p_sb", A_G2 + 4 * K, [P, 2, 2, 256])
        pT = at("pT", A_G2 + 8 * K, [P, 2, 4, P])
        k96 = at("k96", A_G3, [P, TT, M_H, QK])
        nbc = at("nbc", A_MQK, [P, Q_LORA + KV_LORA])
        o_sb = at("o_sb", A_G3, [P, 4, NA_W])
        v_m = at("v_m", A_VM, [P, TT, NA_W])
        mqT = at("mqT", A_MQK, [QK, M_H, TT * P])
        mkT = at("mkT", A_MQK + 8 * K, [QK, M_H, TT * P])
        oT = at("oT", A_MQK, [P, 8, TT * P])
        gates = at("gates", A_GATE, [P, TT, 2 * D])
        tab = at("tab", A_TAB, [P, NA_H, 6, GRID])
        acc = at("acc", A_ADA, [P, 2, D])
        tab_back = at("tab_back", A_G2, [P, NA_H, 6, GRID])
        flip = at("flip", A_MQK + 4 * K, [P, P])
        rope_s = at("rope_s", A_H + 6 * K, [P, 4, 128])
        wr = at("wr", A_TAB, [P, KD, NE])
        brc = at("brc", A_TAB + K, [P, NE])
        rt = at("rt", A_TAB + K + 128, [P, 16, NE])
        m8 = at("m8", A_TAB + 3 * K + 256, [P, TT, 8])
        gT = at("gT", A_TAB + 3 * K + 512, [NE, TT * P])
        b2sb = at("b2sb", A_G2, [NE, D])

        whi = at("whi", 0, [P, SPLITS, UNIT], F32R)
        wlo = at("wlo", 24 * K, [P, SPLITS, UNIT], F32R)
        hs = at("hs", 48 * K, [P, UNIT])
        hb = at("hb", 56 * K, [P, 4, 2, 2 * P])
        sg = at("sg", 64 * K, [P, 4, 2 * P])
        u1 = at("u1", 68 * K, [P, KD, P], F32R)
        u2 = at("u2", 72 * K, [P, KD, P], F32R)
        ys = at("ys", 76 * K, [P, D])
        scS = at("scS", 80 * K, [P, 10])
        scW = at("scW", 80 * K + 64, [P, 10])
        b1c = at("b1c", 80 * K + 128, [P, 16])
        sel_t = at("sel_t", 80 * K + 512, [P, TT, P], F32R)
        sela_t = at("sela_t", 81 * K + 512, [P, TT, P], F32R)
        wsel = at("wsel", 82 * K + 512, [P, TT, P])
        fmat = at("fmat", 83 * K + 512, [P, P])
        tmpP = at("tmpP", 126 * K + 512, [P, P])
        t1 = at("t1", 84 * K, [P, 2, KD, P], F32R)
        t2 = at("t2", 92 * K, [P, 2, KD, P], F32R)
        xs_hi = at("xs_hi", A_GATE, [P, TT, KD, P], F32R)
        xs_lo = at("xs_lo", A_GATE + 8 * K, [P, TT, KD, P], F32R)
        wT = at("wT", 127 * K, [P, TT * P])
        out_acc = at("out_acc", A_ADA, [P, TT, D])
        y_out = at("y_out", 0, [P, TT, D])

        ps = [ctx.enter_context(nc.psum_tensor(f"bank{i}", [P, BANK], F32)) for i in range(8)]

        saved_x = nc.dram_tensor("saved_x", [P, TT, D], F32, kind="Internal").ap()
        saved_g = nc.dram_tensor("saved_g", [P, D], F32, kind="Internal").ap()

        landed = [sem(f"landed{i}") for i in range(SLOTS)]
        x_in, c_in, con_in, rpb_in, nbc_in = (sem(n) for n in ("x_in", "c_in", "con_in", "rpb_in", "nbc_in"))
        gain_pre_in, gain_post_in = sem("gain_pre_in"), sem("gain_post_in")
        bgate_in, b1_in, router_in, b2_in = (sem(n) for n in ("bgate_in", "b1_in", "router_in", "b2_in"))
        ada_row = [sem(f"ada_row{i}") for i in range(2)]
        x_saved, g_saved, back_in, stored = (sem(n) for n in ("x_saved", "g_saved", "back_in", "stored"))
        full_f, out_act, out_dve = sem("front_full"), sem("front_act"), sem("front_dve")
        pe_used, ada_used, head_scored = sem("pe_used"), sem("ada_used"), sem("head_scored")
        acc_clear, acc_made = sem("acc_clear"), sem("acc_made")
        csig, sc_made, ms, var, rstd = (sem(n) for n in ("csig", "sc_made", "ms", "var", "rstd"))
        lat_made, krope, qrope, dve_q = (sem(n) for n in ("lat_made", "krope", "qrope", "dve_q"))
        pool_q, h_made, negmax, exps, pv = (sem(n) for n in ("pool_q", "h_made", "negmax", "exps", "pv"))
        sig_made, merged_s, x1_made, h2_made, xhi_made, xlo_made = (
            sem(n) for n in ("sig_made", "merged", "x1_made", "h2_made", "xhi_made", "xlo_made"))
        nv1, ex_made, mask_made, gate_made, tabs_made, fin = (
            sem(n) for n in ("nv1", "ex_made", "mask_made", "gate_made", "tabs_made", "fin"))
        hi_ready, lo_dve, lo_pool, split_used = (sem(n) for n in ("hi_ready", "lo_dve", "lo_pool", "split_used"))
        misc_full, drain_act, drain_dve = sem("misc_full"), sem("drain_act"), sem("drain_dve")
        hs_act, hs_dve, sel_made, w_made, fold_made, par_made = (
            sem(n) for n in ("hs_act", "hs_dve", "sel_made", "w_made", "fold_made", "par_made"))
        glu_made, lin_made, sg_made, a1_made, a_made, u1_made, u2_made, u_ready, ys_made = (
            sem(n) for n in ("glu_made", "lin_made", "sg_made", "a1_made", "a_made", "u1_made", "u2_made", "u_ready", "ys_made"))
        pool_m, gates_joined, picked = sem("pool_m"), sem("gates_joined"), sem("picked")

        def unit_index(*name):
            return next(n for n, u in enumerate(units) if u[:-1] == name)

        def unit_at(*name):
            return ring[:, unit_index(*name) % SLOTS, :]

        def arrived(eng, *name):
            n = unit_index(*name)
            eng.wait_ge(landed[n % SLOTS], 16 * (n // SLOTS + 1))

        def filled(eng, *key):
            if key[0] == "o":
                eng.wait_ge(pv, 4 * key[1] + 4)
            else:
                eng.wait_ge(full_f, table[key][0])

        def drained(eng, *key):
            _, _, _, who, count = table[key]
            eng.wait_ge(out_act if who == "act" else out_dve, count)

        def bank(*key):
            return ps[table[key][1]]

        def open_bank(pe, *key):
            before = table[key][2]
            if before is not None:
                drained(pe, *before)
            return bank(*key)

        order = {"act": [k for k, g in jobs if g == "act"], "dve": [k for k, g in jobs if g == "dve"]}

        def take(eng, who, *key):
            assert order[who].pop(0) == key, key
            filled(eng, *key)
            return bank(*key)

        def front_source(name):
            n = name[0]
            if n == "ada":
                _, v, u, _ = name
                s = w_ada[0].rearrange("(p k) n -> p k n", k=KD)[:, 2 * u:2 * u + 2, v * D:(v + 1) * D]
                return s, 2, D
            if n in ("q", "k", "v", "gate"):
                u = name[-2]
                c0 = {"q": 0, "k": NA_W, "v": 2 * NA_W}.get(n)
                if n == "gate":
                    c0 = 3 * NA_W + LAT + name[1] * BANK
                return w_in[0].rearrange("(k p) n -> p k n", p=P)[:, 4 * u:4 * u + 4, c0:c0 + BANK], 4, BANK
            if n == "lat":
                k0, k1 = 3 * name[1], min(KD, 3 * name[1] + 3)
                c0 = 3 * NA_W
                return w_in[0].rearrange("(k p) n -> p k n", p=P)[:, k0:k1, c0:c0 + LAT], k1 - k0, LAT
            if n == "uq":
                k0, k1 = (0, 2) if name[1] == 0 else (2, 3)
                return w_uq[0].rearrange("(k p) h d -> p k (h d)", p=P)[:, k0:k1], k1 - k0, M_H * QK
            if n == "ukv":
                return w_ukv[0].rearrange("(k p) h d -> p k (h d)", p=P), 2, D
            if n == "up":
                w = (w_na_up, w_mla_up)[name[1]]
                return w[0].rearrange("(k p) n -> p k n", p=P)[:, 2 * name[2]:2 * name[2] + 2], 2, D
            return w_out[0].rearrange("(k p) n -> p k n", p=P)[:, 2 * name[1]:2 * name[1] + 2], 2, D

        def wait_lo(eng, count, r):
            by_pool, n = count
            eng.wait_ge(lo_pool if by_pool else lo_dve, n + r * (UNITS // 4 if by_pool else 3 * UNITS // 4))

        def over_experts(eng, step):
            step(0, 0)
            step(1, 1)
            with eng.Fori(1, NE // 2 - 1) as i:
                step(2 * i, 0)
                step(2 * i + 1, 1)
            step(NE - 2, 0)
            step(NE - 1, 1)

        def two_sweeps(eng, sweep, between=None, after=None):
            sweep(0)
            eng.wait_ge(tabs_made, 1)
            more = eng.value_load(ovf_i[0:1, 0:1], min_val=0, max_val=TT * P)
            with eng.If(more > full):
                if between:
                    between()
                sweep(1)
                if after:
                    after()
                eng.drain()

        def over_experts_i(eng, step, pair_of):
            step(0, 0)
            step(1, 1)
            with eng.Fori(1, NE // 2 - 1) as i:
                pair_of["i"] = i
                step(2 * i, 0)
                step(2 * i + 1, 1)
            pair_of["i"] = None
            step(NE - 2, 0)
            step(NE - 1, 1)

        block = ctx.enter_context(nc.Block())

        @block.sync
        def _(sp):
            sp.dma_start(st[:, 0:8], c[0].rearrange("(p k) -> p k", k=KD)).then_inc(c_in, 16)
            sp.dma_start(xt[:], x[0].rearrange("(t p) n -> p t n", p=P)).then_inc(x_in, 16)
            sp.dma_start(con[:], consts[:, 0:C_ALL]).then_inc(con_in, 16)
            sp.dma_start(flip[:], consts[:, C_FLIP:C_FLIP + P]).then_inc(con_in, 16)

            def read_before(n):
                who = units[n][-1]
                if who in ("dve", "pe"):
                    sp.wait_ge(ada_used if who == "dve" else pe_used, sum(u[-1] == who for u in units[:n + 1]))
                else:
                    filled(sp, *who)

            for n, name in enumerate(units):
                if n >= SLOTS:
                    read_before(n - SLOTS)
                src, k, cols = front_source(name)
                dst = ring[:, n % SLOTS, 0:k * cols].rearrange("p (k n) -> p k n", k=k)
                sp.dma_start(dst, src).then_inc(landed[n % SLOTS], 16)

            w1_v = w1[0].rearrange("e (p k) n -> e p k n", k=KD)
            w2_v = w2[0].rearrange("e (p k) n -> e p k n", k=KD)

            def w1_unit(e, k, slot):
                sp.dma_start(ring[:, slot, :], w1_v[e, :, k, :]).then_inc(landed[slot], 16)

            def load(e, b, j):
                slot = ring_slot(e, b, j, NF)
                if j < 8:
                    w1_unit(e + j // 4, (j + 4) % 8, slot)
                else:
                    sp.dma_start(ring[:, slot, :].rearrange("p (k n) -> p k n", k=2),
                                 w2_v[e, :, 2 * (j - 8):2 * (j - 8) + 2, :]).then_inc(landed[slot], 16)

            def sweep(r):
                def slot_read(e, j):
                    if isinstance(e, int):
                        m = unit_no(e, j) - SLOTS
                        if m >= 0:
                            wait_lo(sp, lo_count_of_unit(m), r)
                        elif r:
                            wait_lo(sp, lo_count_of_unit(m + UNITS), r - 1)
                        else:
                            read_before(NF + m)
                    else:
                        wait_lo(sp, lo_count(e, j - 8) if j >= 8 else lo_count(e - 1, j + 4), r)

                for m in range(4):
                    if r:
                        wait_lo(sp, lo_count_of_unit(UNITS + m - SLOTS), r - 1)
                    else:
                        read_before(NF + m - SLOTS)
                    w1_unit(0, m, (NF + m) % SLOTS)

                def step(e, b):
                    for j in range(12):
                        if last(e) and 4 <= j < 8:
                            continue
                        slot_read(e, j)
                        load(e, b, j)

                over_experts(sp, step)

            def both_split():
                sp.wait_ge(lo_dve, 2 * 3 * UNITS // 4)
                sp.wait_ge(lo_pool, 2 * UNITS // 4)

            two_sweeps(sp, sweep, after=both_split)
            sp.wait_ge(lo_dve, 3 * UNITS // 4)
            sp.wait_ge(lo_pool, UNITS // 4)
            sp.wait_ge(x_saved, 16)
            sp.wait_ge(g_saved, 16)
            sp.dma_start(ring[:, 0, :], saved_x.rearrange("p t n -> p (t n)")).then_inc(back_in, 16)
            sp.dma_start(ring[:, 1, 0:D], saved_g).then_inc(back_in, 16)
            for tt in range(TT):
                sp.wait_ge(fin, tt + 1)
                sp.dma_start(out[0, tt * P:(tt + 1) * P, :], y_out[:, tt, :]).then_inc(stored, 16)
            sp.wait_ge(stored, 16 * TT)

        @block.gpsimd
        def _(pool):
            rpb = na_rpb[0]
            for par in range(2):
                for hd in range(NA_H):
                    src = bass.AP(rpb.tensor, rpb.offset + hd * RPB_R * RPB_C + (5 - par) * RPB_C + 16 - GRID,
                                  [[1, GRID], [RPB_C, 6], [1, GRID]])
                    pool.dma_start(tab_back[par * GRID:(par + 1) * GRID, hd], src).then_inc(rpb_in, 16)
            pool.dma_start(gbc[:, 0, :], g_attn_pre.to_broadcast([P, D])).then_inc(gain_pre_in, 16)
            pool.dma_start(gbc[:, 1, :], g_attn_post.to_broadcast([P, D])).then_inc(gain_post_in, 16)
            pool.dma_start(nbc[:, 0:Q_LORA], q_norm_g.to_broadcast([P, Q_LORA])).then_inc(nbc_in, 16)
            pool.dma_start(nbc[:, Q_LORA:], kv_norm_g.to_broadcast([P, KV_LORA])).then_inc(nbc_in, 16)

            def start_acc(i):
                v = (0, 1, *ADA_LATE)[i]
                if i >= 2:
                    filled(pool, "mod", (0, 1, *ADA_LATE)[i - 2], 1)
                pool.memset(acc[:, i % 2, :], 0.0).then_inc(acc_clear, 1)
                pool.wait_ge(acc_clear, i + 1)
                pool.dma_start(acc[0:1, i % 2, :], b_ada[:, v * D:(v + 1) * D]).then_inc(ada_row[i % 2], 16)

            start_acc(0)
            start_acc(1)
            for tt in range(TT):
                pool.dma_start(gates[:, tt, :], b_gate.to_broadcast([P, 2 * D])).then_inc(bgate_in, 16)
            pool.dma_start(b1t[:], b1[0].rearrange("e (p q) -> p e q", p=P)).then_inc(b1_in, 16)
            pool.wait_ge(con_in, 32)
            pool.memset(ptab[:], 0.0).then_inc(pool_q, 1)
            seq = [1]

            def link(ins):
                seq[0] += 1
                ins.then_inc(pool_q, 1)
                pool.wait_ge(pool_q, seq[0])

            def rope(view, heads, tt):
                xv = view.rearrange("p h (a s f) -> p h a s f", a=2, s=2)
                x1v, x2v = xv[:, :, :, 0, :], xv[:, :, :, 1, :]
                n = heads * 16
                tb = [con[:, o + 16 * tt:o + 16 * tt + 16].rearrange("p (a f) -> p a f", a=2).unsqueeze(1)
                      .to_broadcast([P, heads, 2, 8]) for o in (C_COS, C_SIN)]
                t4 = [rope_s[:, i, 0:n].rearrange("p (h a f) -> p h a f", a=2, f=8) for i in range(4)]
                pool.tensor_tensor(t4[0], x1v, tb[0], ALU.mult)
                pool.tensor_tensor(t4[1], x2v, tb[1], ALU.mult)
                pool.tensor_tensor(t4[2], x1v, tb[1], ALU.mult)
                link(pool.tensor_tensor(t4[3], x2v, tb[0], ALU.mult))
                pool.tensor_tensor(x1v, t4[0], t4[1], ALU.subtract)
                return pool.tensor_tensor(x2v, t4[2], t4[3], ALU.add)

            for tt in range(TT):
                drained(pool, "lat", tt, 1)
                link(rope(lat[:, tt, Q_LORA + KV_LORA:LAT].unsqueeze(1), 1, tt))
                pool.tensor_copy(k96[:, tt, :, NOPE:QK], lat[:, tt, Q_LORA + KV_LORA:LAT].unsqueeze(1)
                                 .to_broadcast([P, M_H, ROPE])).then_inc(krope, 1)
            for tt in range(TT):
                drained(pool, "uq", tt, 1)
                rope(qm[:, tt, :].rearrange("p (h d) -> p h d", d=QK)[:, :, NOPE:QK], M_H, tt).then_inc(qrope, 1)
                pool.wait_ge(qrope, tt + 1)
            for i in range(2, 6):
                start_acc(i)
                if i == 2:
                    filled(pool, "hT", 0, 0)
                    pool.dma_start(gbc[:, 0, :], g_ffn_pre.to_broadcast([P, D])).then_inc(gain_pre_in, 16)
                if i == 4:
                    drained(pool, "mod", 2, 1)
                    pool.dma_start(gbc[:, 1, :], g_ffn_post.to_broadcast([P, D])).then_inc(gain_post_in, 16)
            pool.wait_ge(exps, 16)
            pool.wait_ge(pv, 16)
            pool.wait_ge(negmax, 16)
            pool.dma_start(wr[:], w_router[0].rearrange("(k p) e -> p k e", p=P)).then_inc(router_in, 16)
            pool.dma_start(brc[:], b_router.to_broadcast([P, NE])).then_inc(router_in, 16)
            pool.dma_start(b2sb[:], b2[0]).then_inc(b2_in, 16)
            pool.wait_ge(x1_made, 2)
            pool.dma_start(saved_x, xt[:]).then_inc(x_saved, 16)
            drained(pool, "mod", 5, 1)
            pool.dma_start(saved_g, modv[:, 1, :]).then_inc(g_saved, 16)
            pool.wait_ge(b1_in, 16)

            def lo_part(e, b, j, r):
                m = unit_no(e, j) + r * UNITS
                pool.wait_ge(hi_ready, m + 1)
                if not (isinstance(m, int) and m < SPLITS):
                    pool.wait_ge(split_used, m + 1 - SPLITS)
                q, s = split_slot(e, j), ring_slot(e, b, j, NF)
                pool.tensor_tensor(wlo[:, q], ring[:, s], whi[:, q].bitcast(F32), ALU.subtract).then_inc(lo_pool, 1)

            def sweep(r):
                def own(ins, value):
                    ins.then_inc(pool_m, 1)
                    pool.wait_ge(pool_m, value)
                    apart()

                def apart():
                    pool.nop(nofuse=True)

                def selection(e, first):
                    n0 = first
                    own(pool.tensor_copy(scS[:], ptab[:, e, :] if isinstance(e, int) else ptab[:, bass.ds(e, 1), :].squeeze(1)), n0 + 1)
                    for tt in range(TT):
                        pos, a, na = (scS[:, 5 * tt + q:5 * tt + q + 1] for q in range(3))
                        pool.tensor_scalar(sel_t[:, tt], iota, pos, na, ALU.is_equal, ALU.mult)
                        own(pool.tensor_scalar(sela_t[:, tt], iota_mod, pos, a, ALU.is_equal, ALU.mult), n0 + 2 + tt)
                        ins = pool.tensor_tensor(sel_t[:, tt, 0:HALF], sel_t[:, tt, 0:HALF].bitcast(F32),
                                                 sela_t[:, tt, 0:HALF].bitcast(F32), ALU.add)
                    ins.then_inc(sel_made, 1)
                    pool.wait_ge(sel_made, r * NE + e + 1)

                def spread(e, first):
                    row = (lambda t: t[:, e, :]) if isinstance(e, int) else (lambda t: t[:, bass.ds(e, 1), :].squeeze(1))
                    pool.tensor_copy(b1c[:], row(b1t))
                    pool.tensor_copy(scW[:], row(ptab)).then_inc(par_made, 1)
                    pool.wait_ge(par_made, r * NE + e + 1)
                    apart()
                    own(pool.tensor_scalar(tmpP[:], offdiag, scW[:, 1:2], None, ALU.mult), first + 1)
                    pool.tensor_tensor(fmat[:], tmpP[:], ident, ALU.add).then_inc(fold_made, 1)
                    pool.wait_ge(fold_made, r * NE + e + 1)
                    apart()
                    for tt in range(TT):
                        pos, ga, gb = (scW[:, 5 * tt + q:5 * tt + q + 1] for q in (0, 3, 4))
                        pool.tensor_scalar(tmpP[:], iota_mod, pos, ga, ALU.is_equal, ALU.mult)
                        own(pool.tensor_scalar(wsel[:, tt], iota, pos, gb, ALU.is_equal, ALU.mult), first + 2 + 2 * tt)
                        ins = pool.tensor_tensor(wsel[:, tt], wsel[:, tt], tmpP[:], ALU.add)
                        if tt == 0:
                            own(ins, first + 3)
                    ins.then_inc(w_made, 1)
                    pool.wait_ge(w_made, r * NE + e + 1)

                SEL, SPR = 3, 4
                b0 = r * (SEL * NE + SPR * NE)
                fb = r * FILLS
                if r == 0:
                    pool.wait_ge(tabs_made, 1)
                else:
                    pool.wait_ge(tabs_made, 2)
                    pool.wait_ge(misc_full, FILLS)
                selection(0, b0)
                pool.wait_ge(misc_full, fb + 4)
                selection(1, b0 + SEL)
                pool.wait_ge(hi_ready, r * UNITS + 3)
                if r:
                    pool.wait_ge(split_used, r * UNITS + 3 - SPLITS)
                pool.tensor_tensor(wlo[:, 2], ring[:, (NF + 2) % SLOTS], whi[:, 2].bitcast(F32),
                                   ALU.subtract).then_inc(lo_pool, 1)

                def step(e, b):
                    own0 = b0 + 2 * SEL + (SEL + SPR) * e - (SEL if last(e) else 0)
                    lo_part(e, b, 2, r)
                    if not no_gather(e):
                        if isinstance(e, int) and e == 0:
                            pool.wait_ge(misc_full, fb + PRE_FILLS)
                        else:
                            pool.wait_ge(misc_full, fb + fill_no(e - 1, "g3") + 1)
                        selection(e + 2, own0)
                        own0 = own0 + SEL
                    if not (isinstance(e, int) and e == 0):
                        pool.wait_ge(misc_full, fb + fill_no(e - 1, "w") + 1)
                        pool.wait_ge(u_ready, r * NE + e)
                        pool.wait_ge(drain_dve, r * DVE_DRAINS + drains(e - 1, "f3")[1])
                    elif r:
                        pool.wait_ge(u_ready, r * NE)
                    spread(e, own0)
                    if not last(e):
                        lo_part(e, b, 6, r)
                    lo_part(e, b, 10, r)

                over_experts(pool, step)

            two_sweeps(pool, sweep)

        @block.scalar
        def _(act):
            act.wait_ge(c_in, 16)
            act.activation(st[:, 8:16], st[:, 0:8], ACT.Sigmoid).then_inc(csig, 1)

            def squares(parts, g):
                for i, (src, junk, width) in enumerate(parts):
                    ins = act.activation(junk, src, ACT.Square, scale=float(width) ** -0.5,
                                         accum_out=st[:, 32 + 4 * g + i:33 + 4 * g + i])
                ins.then_inc(ms, 1)

            def roots(g, n):
                act.wait_ge(var, g + 1)
                act.activation(st[:, 56 + 4 * g:56 + 4 * g + n], st[:, 56 + 4 * g:56 + 4 * g + n], ACT.Sqrt).then_inc(rstd, 1)

            act.wait_ge(x_in, 16)
            squares([(xt[:, tt], h[:, tt], D) for tt in range(TT)], 0)
            roots(0, 2)
            for half in range(2):
                b = take(act, "act", "mod", 0, half)
                act.activation(modv[:, 0, half * BANK:(half + 1) * BANK], b[:], ACT.Copy).then_inc(out_act, 1)
            for tt in range(TT):
                b = take(act, "act", "hT", tt, 0)
                act.activation(hT[:, 0:4, tt * P:(tt + 1) * P], b[:].rearrange("p (c t) -> p c t", c=4), ACT.Copy).then_inc(out_act, 1)
            for tt in range(TT):
                b = take(act, "act", "lat", tt, 1)
                act.activation(lat[:, tt, BANK:LAT], b[:, 0:LAT - BANK], ACT.Copy).then_inc(out_act, 1)
            drained(act, "lat", 0, 0)
            drained(act, "lat", 1, 0)
            drained(act, "lat", 1, 1)
            drained(act, "hT", 1, 1)
            filled(act, "hT", 1, 1)
            squares([(lat[:, tt, 0:Q_LORA], h[:, 0, tt * Q_LORA:(tt + 1) * Q_LORA], Q_LORA) for tt in range(TT)]
                    + [(lat[:, tt, Q_LORA:Q_LORA + KV_LORA], h[:, tt, (1 - tt) * 2 * Q_LORA:][:, 0:KV_LORA], KV_LORA) for tt in range(TT)], 1)
            roots(1, 4)
            for name, dst in (("q", qT), ("k", kT)):
                for cc in range(4):
                    b = take(act, "act", name, cc)
                    act.activation(dst[:, cc, :], b[:, 0:TT * P], ACT.Copy).then_inc(out_act, 1)
            for tt in range(TT):
                b = take(act, "act", "ckT", tt)
                act.activation(cT[:, 3:5, tt * P:(tt + 1) * P], b[:, 0:2 * P].rearrange("p (c t) -> p c t", c=2), ACT.Copy).then_inc(out_act, 1)
            for tt in range(TT):
                for half in range(2):
                    b = take(act, "act", "ukv", tt, half)
                    kv = b[:].rearrange("p (h d) -> p h d", d=P)
                    act.activation(k96[:, tt, 4 * half:4 * half + 4, 0:NOPE], kv[:, :, 0:NOPE], ACT.Copy)
                    act.activation(v_m[:, tt, half * 256:(half + 1) * 256].rearrange("p (h d) -> p h d", d=64),
                                   kv[:, :, NOPE:P], ACT.Copy).then_inc(out_act, 1)
            for tt in range(TT):
                for g in range(2):
                    b = take(act, "act", "mqT", tt, g)
                    act.activation(mqT[:, 4 * g:4 * g + 4, tt * P:(tt + 1) * P], b[0:QK, :].rearrange("p (c t) -> p c t", c=4), ACT.Copy).then_inc(out_act, 1)

            def softmax(n):
                act.wait_ge(negmax, n + 1)
                if n >= 2:
                    filled(act, "pT", n - 2)
                for hh in range(2):
                    ins = act.activation(p_sb[:, n % 2, hh], s_sb[:, n % 2, hh], ACT.Exp,
                                         bias=nmx[:, n % 2, hh:hh + 1], accum_out=lsum[:, 2 * n + hh:2 * n + hh + 1])
                ins.then_inc(exps, 1)

            softmax(0)
            softmax(1)
            for n in range(16):
                if n >= 2:
                    act.wait_ge(pv, n - 1)
                b = take(act, "act", "pT", n)
                act.activation(pT[:, n % 2], b[:].rearrange("p (c t) -> p c t", c=4), ACT.Copy).then_inc(out_act, 1)
                if n + 2 < 16:
                    softmax(n + 2)
                if MOD_AFTER.get(n) == 3:
                    for half in range(2):
                        b = take(act, "act", "mod", 3, half)
                        act.activation(modv[:, 0, half * BANK:(half + 1) * BANK], b[:], ACT.Copy).then_inc(out_act, 1)
            drained(act, "gate", 3, 1)
            act.activation(gates[:], gates[:], ACT.Sigmoid).then_inc(sig_made, 1)
            for a in (0, 2):
                b = take(act, "act", "oT", a)
                act.activation(oT[:, 4 * (a // 2):4 * (a // 2) + 4, (a % 2) * P:(a % 2 + 1) * P],
                               b[:].rearrange("p (c t) -> p c t", c=4), ACT.Copy).then_inc(out_act, 1)
            for tt in range(TT):
                b = take(act, "act", "mT", tt, 0)
                act.activation(hT[:, 0:4, tt * P:(tt + 1) * P], b[:].rearrange("p (c t) -> p c t", c=4), ACT.Copy).then_inc(out_act, 1)
            for tt in range(TT):
                for half in range(2):
                    b = take(act, "act", "y", tt, half)
                    act.activation(ysb[:, tt, half * BANK:(half + 1) * BANK], b[:], ACT.Copy).then_inc(out_act, 1)
            drained(act, "y", 1, 1)
            squares([(ysb[:, tt], h[:, tt], D) for tt in range(TT)], 2)
            roots(2, 2)
            act.wait_ge(x1_made, 2)
            squares([(xt[:, tt], h[:, tt], D) for tt in range(TT)], 3)
            roots(3, 2)
            for tt in range(TT):
                b = take(act, "act", "h2T", tt, 0)
                act.activation(hT[:, 0:4, tt * P:(tt + 1) * P], b[:].rearrange("p (c t) -> p c t", c=4), ACT.Copy).then_inc(out_act, 1)
            act.wait_ge(h2_made, 2)
            for tt in range(TT):
                act.activation(xs_hi[:, tt], h[:, tt, :].rearrange("p (q k) -> p k q", k=KD), ACT.Copy).then_inc(xhi_made, 1)
            act.wait_ge(nv1, 2)
            for tt in range(TT):
                ins = act.activation(rt[:, 2 + tt], rt[:, tt], ACT.Exp, bias=st[:, 80 + tt:81 + tt])
            ins.then_inc(ex_made, 1)
            for tt in range(TT):
                for half in range(2):
                    b = take(act, "act", "b2", tt, half)
                    act.activation(out_acc[:, tt, half * BANK:(half + 1) * BANK], b[:], ACT.Copy).then_inc(out_act, 1)
            act.wait_ge(x_saved, 16)
            act.wait_ge(g_saved, 16)
            act.wait_ge(xlo_made, 2)

            def hi_part(e, b, j, r, pair=None):
                m = unit_no(e, j)
                if isinstance(m, int):
                    n = NF + m + r * UNITS
                    act.wait_ge(landed[n % SLOTS], 16 * (n // SLOTS + 1))
                    slot = n % SLOTS
                else:
                    slot = ring_slot(e, b, j, NF)
                    n0 = NF + 4 + 12 * b + j + r * UNITS
                    act.wait_ge(landed[slot], 48 * pair + 16 * (n0 // SLOTS + 1))
                q = split_slot(e, j)
                if not (isinstance(m, int) and r == 0 and m < SPLITS):
                    act.wait_ge(split_used, m + r * UNITS + 1 - SPLITS)
                act.activation(whi[:, q], ring[:, slot], ACT.Copy).then_inc(hi_ready, 1)

            pair_of = {"i": None}

            def sweep(r):
                fb, ab = r * FILLS, r * ACT_DRAINS

                def drain_gather(fill, which_bank, q, par):
                    act.wait_ge(misc_full, fill + 1)
                    t, half = (t1, t2)[q // 2], q % 2
                    act.activation(t[:, par, 4 * half:4 * half + 4], ps[6 + which_bank][:].rearrange("p (c t) -> p c t", c=4), ACT.Copy).then_inc(drain_act, 1)

                for par in range(2):
                    for q in range(4):
                        drain_gather(fb + 4 * par + q, q % 2, q, par)
                for m in range(4):
                    n = NF + m + r * UNITS
                    act.wait_ge(landed[n % SLOTS], 16 * (n // SLOTS + 1))
                    if m + r * UNITS >= SPLITS:
                        act.wait_ge(split_used, m + r * UNITS + 1 - SPLITS)
                    act.activation(whi[:, m % SPLITS], ring[:, n % SLOTS], ACT.Copy).then_inc(hi_ready, 1)
                hi_part(0, 0, 0, r)

                def step(e, b):
                    f0 = fb + fills_before(e)
                    par = (e if isinstance(e, int) else b) % 2
                    for j in (1, 2, 3):
                        hi_part(e, b, j, r, pair_of["i"])
                    if not last(e):
                        hi_part(e, b, 4, r, pair_of["i"])
                    act.wait_ge(split_used, r * UNITS + unit_no(e, 3) + 1)
                    for q in range(2):
                        ins = act.activation(hs[:, q * BANK:(q + 1) * BANK], ps[q][:], ACT.Copy)
                    ins.then_inc(hs_act, 1)
                    if not last(e):
                        hi_part(e, b, 5, r, pair_of["i"])
                    if not no_gather(e):
                        for q in range(4):
                            drain_gather(f0 + q, bank_of(e, "g%d" % q, b), q, par)
                    if not last(e):
                        hi_part(e, b, 6, r, pair_of["i"])
                    act.wait_ge(glu_made, r * NE + e + 1)
                    act.activation(sg[:], hb[:, :, 0, :], ACT.Sigmoid, scale=ALPHA).then_inc(sg_made, 1)
                    if not last(e):
                        hi_part(e, b, 7, r, pair_of["i"])
                    act.wait_ge(a_made, r * NE + e + 1)
                    if not (isinstance(e, int) and e == 0 and r == 0):
                        prev = unit_no(e - 1, 11) if not (isinstance(e, int) and e == 0) else -1
                        act.wait_ge(split_used, r * UNITS + prev + 1)
                    act.activation(u1[:].rearrange("p k t -> p (k t)"), sg[:].rearrange("p f t -> p (f t)"), ACT.Copy).then_inc(u1_made, 1)
                    hi_part(e, b, 8, r, pair_of["i"])
                    act.wait_ge(misc_full, fb + fill_no(e, "w") + 1)
                    act.activation(wT[:], ps[6 + bank_of(e, "w", b)][:, 0:TT * P], ACT.Copy).then_inc(drain_act, 1)
                    for j in (9, 10, 11):
                        hi_part(e, b, j, r, pair_of["i"])
                    if not last(e):
                        hi_part(e + 1, 1 - b, 0, r, None if pair_of["i"] is None else pair_of["i"] + b)
                    act.wait_ge(split_used, r * UNITS + unit_no(e, 11) + 1)
                    for q in range(2):
                        ins = act.activation(ys[:, q * BANK:(q + 1) * BANK], ps[4 + q][:], ACT.Copy)
                    ins.then_inc(ys_made, 1)

                over_experts_i(act, step, pair_of)

            two_sweeps(act, sweep, after=lambda: act.wait_ge(drain_dve, 2 * DVE_DRAINS))
            act.wait_ge(drain_dve, DVE_DRAINS)
            act.wait_ge(a_made, NE)
            squares([(out_acc[:, tt], hs[:, 0:D] if tt == 0 else hs[:, D:2 * D], D) for tt in range(TT)], 4)
            roots(4, 2)

        @block.vector
        def _(dve):
            seq = [0]

            def link(ins):
                seq[0] += 1
                ins.then_inc(dve_q, 1)
                dve.wait_ge(dve_q, seq[0])

            dve.wait_ge(csig, 1)
            link(dve.tensor_tensor(st[:, 16:24], st[:, 0:8], st[:, 8:16], ALU.mult))

            def ada_unit(i, u):
                v = (0, 1, *ADA_LATE)[i]
                arrived(dve, "ada", v, u)
                if u == 0:
                    dve.wait_ge(ada_row[i % 2], 16 * (i // 2 + 1))
                src = unit_at("ada", v, u).rearrange("p (k n) -> p k n", k=2)
                for q in range(2):
                    k = 2 * u + q
                    ins = dve.scalar_tensor_tensor(acc[:, i % 2], src[:, q], st[:, 16 + k:17 + k], acc[:, i % 2], ALU.mult, ALU.add)
                    if q == 0:
                        link(ins)
                ins.then_inc(ada_used, 1)
                dve.wait_ge(ada_used, 4 * i + u + 1)

            def inverse(g, n):
                dve.wait_ge(ms, g + 1)
                link(dve.tensor_scalar(st[:, 32 + 4 * g:32 + 4 * g + n], st[:, 32 + 4 * g:32 + 4 * g + n], EPS, None, ALU.add))
                dve.reciprocal(st[:, 56 + 4 * g:56 + 4 * g + n], st[:, 32 + 4 * g:32 + 4 * g + n]).then_inc(var, 1)

            def root(g, i):
                return st[:, 56 + 4 * g + i:57 + 4 * g + i]

            def mod_drain(v):
                for half in range(2):
                    b = take(dve, "dve", "mod", v, half)
                    dst, gain = modv[:, MODV[v], half * BANK:(half + 1) * BANK], gbc[:, 1 if v in (2, 5) else 0, half * BANK:(half + 1) * BANK]
                    if v in (1, 4):
                        dve.scalar_tensor_tensor(dst, b[:], 1.0, gain, ALU.add, ALU.mult).then_inc(out_dve, 1)
                    else:
                        dve.tensor_tensor(dst, b[:], gain, ALU.mult).then_inc(out_dve, 1)

            inverse(0, 2)
            dve.wait_ge(con_in, 32)
            mask = con[:, C_MASK:C_MASK + GRID].unsqueeze(1).to_broadcast([P, BANK // GRID, GRID])
            tab_rows = tab[:].rearrange("p h r c -> p (h r) c")
            for i in range(NA_H * 6 * GRID // BANK):
                b = take(dve, "dve", "tab", i)
                dve.tensor_tensor(tab_rows[:, i * (BANK // GRID):(i + 1) * (BANK // GRID)], b[:].rearrange("p (r c) -> p r c", c=GRID), mask, ALU.add).then_inc(out_dve, 1)
            for u in range(4):
                ada_unit(0, u)
            for u in range(4):
                ada_unit(1, u)
            dve.wait_ge(gain_pre_in, 16)
            mod_drain(1)
            dve.wait_ge(rstd, 1)
            drained(dve, "mod", 1, 1)
            drained(dve, "mod", 0, 1)

            def norm_in(src, g, shift_sem):
                for tt in range(TT):
                    link(dve.scalar_tensor_tensor(h[:, tt], src[:, tt], root(g, tt), modv[:, MODV[4] if g else MODV[1]], ALU.mult, ALU.mult))
                    dve.tensor_tensor(h[:, tt], h[:, tt], modv[:, 0], ALU.add).then_inc(shift_sem, 1)

            norm_in(xt, 0, h_made)
            for tt in range(TT):
                b = take(dve, "dve", "hT", tt, 1)
                dve.tensor_copy(hT[:, 4:8, tt * P:(tt + 1) * P], b[:].rearrange("p (c t) -> p c t", c=4)).then_inc(out_dve, 1)
            for tt in range(TT):
                b = take(dve, "dve", "lat", tt, 0)
                dve.tensor_copy(lat[:, tt, 0:BANK], b[:]).then_inc(out_dve, 1)
            inverse(1, 4)
            dve.wait_ge(rstd, 2)
            dve.wait_ge(nbc_in, 32)
            for tt in range(TT):
                a, z = lat[:, tt, 0:Q_LORA], lat[:, tt, Q_LORA:Q_LORA + KV_LORA]
                dve.scalar_tensor_tensor(a, a, root(1, tt), nbc[:, 0:Q_LORA], ALU.mult, ALU.mult)
                dve.scalar_tensor_tensor(z, z, root(1, 2 + tt), nbc[:, Q_LORA:], ALU.mult, ALU.mult).then_inc(lat_made, 1)
            for tt in range(TT):
                b = take(dve, "dve", "v", tt)
                dve.tensor_copy(v_na[:, tt], b[:]).then_inc(out_dve, 1)
            for tt in range(TT):
                b = take(dve, "dve", "cqT", tt)
                dve.tensor_copy(cT[:, 0:3, tt * P:(tt + 1) * P], b[:, 0:3 * P].rearrange("p (c t) -> p c t", c=3)).then_inc(out_dve, 1)
            for tt in range(TT):
                for half in range(2):
                    b = take(dve, "dve", "uq", tt, half)
                    dve.tensor_copy(qm[:, tt, half * 384:(half + 1) * 384], b[:, 0:384]).then_inc(out_dve, 1)
            for tt in range(TT):
                for g in range(2):
                    b = take(dve, "dve", "mkT", tt, g)
                    dve.tensor_copy(mkT[:, 4 * g:4 * g + 4, tt * P:(tt + 1) * P], b[0:QK, :].rearrange("p (c t) -> p c t", c=4)).then_inc(out_dve, 1)

            def scores(n):
                br, tt, hp = n // 8, n // 4 % 2, n % 4
                b = take(dve, "dve", "s", n)
                if n >= 2:
                    dve.wait_ge(exps, n - 1)
                if n == 0:
                    drained(dve, "tab", NA_H * 6 * GRID // BANK - 1)
                    filled(dve, "mqT", 1, 1)
                if br == 0:
                    j0 = 2 - 2 * tt
                    ins = dve.scalar_tensor_tensor(s_sb[:, n % 2], b[:].rearrange("p (h k) -> p h k", h=2), NA_D ** -0.5,
                                                   tab[:, 2 * hp:2 * hp + 2, j0:j0 + 4, :].rearrange("p h r c -> p h (r c)"), ALU.mult, ALU.add)
                else:
                    ins = dve.tensor_scalar(s_sb[:, n % 2], b[:].rearrange("p (h k) -> p h k", h=2), QK ** -0.5, None, ALU.mult)
                ins.then_inc(out_dve, 1)
                drained(dve, "s", n)
                link(dve.tensor_reduce(mx[:, n % 2], s_sb[:, n % 2], AX, ALU.max))
                dve.tensor_scalar(nmx[:, n % 2], mx[:, n % 2], -1.0, None, ALU.mult).then_inc(negmax, 1)

            scores(0)
            scores(1)
            for n in range(16):
                ada_unit(2 + n // 4, n % 4)
                if n + 2 < 16:
                    scores(n + 2)
                if n % 4 == 3:
                    a = n // 4
                    dve.wait_ge(exps, n + 1)
                    link(dve.reciprocal(linv[:, 8 * a:8 * a + 8], lsum[:, 8 * a:8 * a + 8]))
                    b = take(dve, "dve", "o", a)
                    dve.tensor_tensor(o_sb[:, a].rearrange("p (h d) -> p h d", d=64), b[:].rearrange("p (h d) -> p h d", d=64),
                                      linv[:, 8 * a:8 * a + 8].unsqueeze(2).to_broadcast([P, 8, 64]), ALU.mult).then_inc(out_dve, 1)
                if n % 4 == 2:
                    if n == 2:
                        dve.wait_ge(bgate_in, 16 * TT)
                    for tt in range(TT):
                        b = take(dve, "dve", "gate", n // 4, tt)
                        g = gates[:, tt, (n // 4) * BANK:(n // 4 + 1) * BANK]
                        dve.tensor_tensor(g, b[:], g, ALU.add).then_inc(out_dve, 1)
                if n in MOD_AFTER and MOD_AFTER[n] != 3:
                    if MOD_AFTER[n] == 4:
                        dve.wait_ge(gain_pre_in, 32)
                    else:
                        dve.wait_ge(gain_post_in, 16 if MOD_AFTER[n] == 2 else 32)
                    mod_drain(MOD_AFTER[n])
            for a in (1, 3):
                b = take(dve, "dve", "oT", a)
                dve.tensor_copy(oT[:, 4 * (a // 2):4 * (a // 2) + 4, (a % 2) * P:(a % 2 + 1) * P],
                                b[:].rearrange("p (c t) -> p c t", c=4)).then_inc(out_dve, 1)
            dve.wait_ge(sig_made, 1)
            for br in range(2):
                for tt in range(TT):
                    for half in range(2):
                        b = take(dve, "dve", "up", br, tt, half)
                        g = gates[:, tt, br * D + half * BANK:br * D + (half + 1) * BANK]
                        m = h[:, tt, half * BANK:(half + 1) * BANK]
                        if br == 0:
                            dve.tensor_tensor(m, b[:], g, ALU.mult).then_inc(out_dve, 1)
                        else:
                            dve.tensor_tensor(g, b[:], g, ALU.mult).then_inc(out_dve, 1)
                            drained(dve, "up", br, tt, half)
                            dve.tensor_tensor(m, m, g, ALU.add).then_inc(merged_s, 1)
            for tt in range(TT):
                b = take(dve, "dve", "mT", tt, 1)
                dve.tensor_copy(hT[:, 4:8, tt * P:(tt + 1) * P], b[:].rearrange("p (c t) -> p c t", c=4)).then_inc(out_dve, 1)
            inverse(2, 2)
            dve.wait_ge(rstd, 3)
            for tt in range(TT):
                link(dve.scalar_tensor_tensor(ysb[:, tt], ysb[:, tt], root(2, tt), modv[:, MODV[2]], ALU.mult, ALU.mult))
                dve.tensor_tensor(xt[:, tt], xt[:, tt], ysb[:, tt], ALU.add).then_inc(x1_made, 1)
            inverse(3, 2)
            dve.wait_ge(rstd, 4)
            drained(dve, "mod", 3, 1)
            norm_in(xt, 3, h2_made)
            for tt in range(TT):
                b = take(dve, "dve", "h2T", tt, 1)
                dve.tensor_copy(hT[:, 4:8, tt * P:(tt + 1) * P], b[:].rearrange("p (c t) -> p c t", c=4)).then_inc(out_dve, 1)
            L, EX, GT, EQ, CUM, MASK, GATE, TMP = 0, 2, 4, 6, 8, 10, 12, 14
            dve.wait_ge(router_in, 32)
            for tt in range(TT):
                b = take(dve, "dve", "lg", tt)
                ins = dve.tensor_tensor(rt[:, L + tt], b[:, 0:NE], brc[:], ALU.add)
                ins.then_inc(out_dve, 1)
                drained(dve, "lg", tt)
                link(dve.max(m8[:, tt], rt[:, L + tt]))
                dve.tensor_scalar(st[:, 80 + tt:81 + tt], m8[:, tt, 0:1], -1.0, None, ALU.mult).then_inc(nv1, 1)
                v4 = m8[:, tt, TOPK - 1:TOPK]
                dve.tensor_scalar(rt[:, GT + tt], rt[:, L + tt], v4, None, ALU.is_gt)
                link(dve.tensor_scalar(rt[:, EQ + tt], rt[:, L + tt], v4, None, ALU.is_equal))
                dve.tensor_reduce(st[:, 82 + tt:83 + tt], rt[:, GT + tt], AX, ALU.add)
                link(dve.tensor_tensor_scan(rt[:, CUM + tt], ones[:, 0:NE], rt[:, EQ + tt], 0.0, ALU.mult, ALU.add))
                link(dve.tensor_scalar(st[:, 84 + tt:85 + tt], st[:, 82 + tt:83 + tt], -1.0, float(TOPK), ALU.mult, ALU.add))
                link(dve.scalar_tensor_tensor(rt[:, CUM + tt], rt[:, CUM + tt], st[:, 84 + tt:85 + tt], rt[:, EQ + tt], ALU.is_le, ALU.mult))
                dve.tensor_tensor(rt[:, MASK + tt], rt[:, GT + tt], rt[:, CUM + tt], ALU.add).then_inc(mask_made, 1)
            dve.wait_ge(mask_made, 2)
            dve.wait_ge(ex_made, 1)
            for tt in range(TT):
                link(dve.tensor_tensor(rt[:, TMP + tt], rt[:, EX + tt], rt[:, MASK + tt], ALU.mult))
                link(dve.tensor_reduce(st[:, 86 + tt:87 + tt], rt[:, TMP + tt], AX, ALU.add))
                link(dve.reciprocal(st[:, 86 + tt:87 + tt], st[:, 86 + tt:87 + tt]))
                dve.tensor_scalar(rt[:, GATE + tt], rt[:, TMP + tt], st[:, 86 + tt:87 + tt], None, ALU.mult).then_inc(gate_made, 1)
            dve.wait_ge(pool_q, 1)
            pt = ptab[:, 0:NE, :]
            for tt in range(TT):
                b = take(dve, "dve", "pos", tt)
                dve.scalar_tensor_tensor(rt[:, EQ + tt], b[:, 0:NE], 1.0, rt[:, MASK + tt], ALU.add, ALU.mult).then_inc(out_dve, 1)
                drained(dve, "pos", tt)
                dve.tensor_scalar(pt[:, :, 5 * tt], rt[:, EQ + tt], -1.0, None, ALU.add)
            b = take(dve, "dve", "cnt")
            dve.tensor_copy(rt[:, TMP], b[:, 0:NE]).then_inc(out_dve, 1)
            drained(dve, "cnt")
            dve.wait_ge(gate_made, 2)
            dve.tensor_copy(cnt_i[:], rt[:, TMP])
            for tt in range(TT):
                dve.tensor_scalar(pt[:, :, 5 * tt + 1], rt[:, TMP], float(half_cap), None, ALU.is_le)
                dve.tensor_scalar(pt[:, :, 5 * tt + 2], rt[:, TMP], float(half_cap), None, ALU.is_gt)
                dve.scalar_tensor_tensor(pt[:, :, 5 * tt + 3], rt[:, TMP], float(half_cap), rt[:, GATE + tt], ALU.is_le, ALU.mult)
                dve.scalar_tensor_tensor(pt[:, :, 5 * tt + 4], rt[:, TMP], float(half_cap), rt[:, GATE + tt], ALU.is_gt, ALU.mult)
            link(dve.tensor_reduce(st[:, 88:89], rt[:, TMP], AX, ALU.max))
            dve.tensor_copy(ovf_i[:], st[:, 88:89]).then_inc(tabs_made, 1)
            for tt in range(TT):
                b = take(dve, "dve", "gT", tt)
                dve.tensor_copy(gT[:, tt * P:(tt + 1) * P], b[0:NE, 0:P]).then_inc(out_dve, 1)
            for tt in range(TT):
                dve.wait_ge(xhi_made, tt + 1)
                dve.tensor_tensor(xs_lo[:, tt], h[:, tt, :].rearrange("p (q k) -> p k q", k=KD), xs_hi[:, tt].bitcast(F32), ALU.subtract).then_inc(xlo_made, 1)
            drained(dve, "b2", 1, 1)

            def lo_part(e, b, j, r):
                m = unit_no(e, j) + r * UNITS
                dve.wait_ge(hi_ready, m + 1)
                if not (isinstance(m, int) and m < SPLITS):
                    dve.wait_ge(split_used, m + 1 - SPLITS)
                q, s = split_slot(e, j), ring_slot(e, b, j, NF)
                dve.tensor_tensor(wlo[:, q], ring[:, s], whi[:, q].bitcast(F32), ALU.subtract).then_inc(lo_dve, 1)

            def sweep(r):
                fb, db, eb = r * FILLS, r * DVE_DRAINS, r * NE
                for m in (0, 1, 3):
                    dve.wait_ge(hi_ready, r * UNITS + m + 1)
                    if m + r * UNITS >= SPLITS:
                        dve.wait_ge(split_used, m + r * UNITS + 1 - SPLITS)
                    dve.tensor_tensor(wlo[:, m % SPLITS], ring[:, (NF + m) % SLOTS], whi[:, m % SPLITS].bitcast(F32), ALU.subtract).then_inc(lo_dve, 1)
                lo_part(0, 0, 0, r)

                def step(e, b):
                    for j in (1, 3):
                        lo_part(e, b, j, r)
                    if not last(e):
                        lo_part(e, b, 4, r)
                    dve.wait_ge(split_used, r * UNITS + unit_no(e, 3) + 1)
                    for q in (2, 3):
                        ins = dve.tensor_copy(hs[:, q * BANK:(q + 1) * BANK], ps[q][:])
                    ins.then_inc(hs_dve, 1)
                    if not last(e):
                        lo_part(e, b, 5, r)
                    dve.wait_ge(par_made, eb + e + 1)
                    if not (isinstance(e, int) and e == 0 and r == 0):
                        dve.wait_ge(u_ready, eb + e)
                        dve.wait_ge(u1_made, eb + e)
                    for f in range(4):
                        dve.wait_ge(misc_full, fb + fill_no(e, "f%d" % f) + 1)
                        bias = b1c[:].rearrange("p (k g) -> p g k", g=2)[:, :, 2 * f:2 * f + 2].unsqueeze(3).to_broadcast([P, 2, 2, P])
                        dve.tensor_tensor(hb[:, f].rearrange("p g (k t) -> p g k t", k=2),
                                          ps[6 + bank_of(e, "f%d" % f, b)][:].rearrange("p (g k t) -> p g k t", g=2, k=2), bias, ALU.add).then_inc(drain_dve, 1)
                    dve.wait_ge(drain_dve, db + drains(e, "f3")[1])
                    glu, lin = hb[:, :, 0, :], hb[:, :, 1, :]
                    dve.tensor_scalar(glu, glu, LIMIT, None, ALU.min).then_inc(glu_made, 1)
                    dve.tensor_scalar(lin, lin, LIMIT, -LIMIT, ALU.min, ALU.max).then_inc(lin_made, 1)
                    if not last(e):
                        lo_part(e, b, 7, r)
                    dve.wait_ge(sg_made, eb + e + 1)
                    dve.tensor_tensor(sg[:], sg[:], glu, ALU.mult).then_inc(a1_made, 1)
                    dve.wait_ge(a1_made, eb + e + 1)
                    dve.wait_ge(lin_made, eb + e + 1)
                    dve.scalar_tensor_tensor(sg[:], lin, 1.0, sg[:], ALU.add, ALU.mult).then_inc(a_made, 1)
                    dve.wait_ge(u1_made, eb + e + 1)
                    u1f, u2f = u1[:].rearrange("p k t -> p (k t)"), u2[:].rearrange("p k t -> p (k t)")
                    dve.tensor_tensor(u2f, sg[:].rearrange("p f t -> p (f t)"), u1f.bitcast(F32), ALU.subtract).then_inc(u2_made, 1)
                    dve.wait_ge(u2_made, eb + e + 1)
                    dve.nop(nofuse=True)
                    a_half = sg[:].rearrange("p f (k t) -> p (f k) t", k=2)[:, :, HALF:P]
                    dve.copy_predicated(a_half, scW[:, 1:2].bitcast(U32).unsqueeze(1).to_broadcast([P, KD, HALF]),
                                        u2[:, :, HALF:P].bitcast(F32)).then_inc(picked, 1)
                    dve.wait_ge(picked, eb + e + 1)
                    dve.tensor_copy(u1[:, :, HALF:P], a_half).then_inc(u_ready, 1)
                    for j in (8, 9, 11):
                        lo_part(e, b, j, r)
                    if not last(e):
                        lo_part(e + 1, 1 - b, 0, r)
                    if not (isinstance(e, int) and e == 0 and r == 0):
                        dve.wait_ge(drain_dve, db + 8 * e)
                    for q in range(4):
                        dve.wait_ge(misc_full, fb + fill_no(e, "c%d" % q) + 1)
                        dst = out_acc[:, q // 2, (q % 2) * BANK:(q % 2 + 1) * BANK]
                        dve.tensor_tensor(dst, ps[6 + bank_of(e, "c%d" % q, b)][:], dst, ALU.add).then_inc(drain_dve, 1)

                over_experts(dve, step)

            def more_positions():
                dve.wait_ge(w_made, NE)
                for tt in range(TT):
                    dve.tensor_scalar(pt[:, :, 5 * tt], pt[:, :, 5 * tt], -float(full), None, ALU.add)
                    dve.tensor_tensor(pt[:, :, 5 * tt + 4], pt[:, :, 5 * tt + 3], pt[:, :, 5 * tt + 4], ALU.add).then_inc(gates_joined, 1)
                dve.wait_ge(gates_joined, TT)
                for tt in range(TT):
                    dve.memset(pt[:, :, 5 * tt + 3], 0.0)
                    dve.memset(pt[:, :, 5 * tt + 1], 0.0)
                    dve.memset(pt[:, :, 5 * tt + 2], 1.0)
                dve.tensor_copy(st[:, 90:91], st[:, 88:89]).then_inc(tabs_made, 1)

            two_sweeps(dve, sweep, more_positions, lambda: dve.wait_ge(drain_dve, 2 * DVE_DRAINS))
            dve.wait_ge(drain_dve, DVE_DRAINS)
            inverse(4, 2)
            dve.wait_ge(rstd, 5)
            dve.wait_ge(back_in, 32)
            res, gf = ring[:, 0, :].rearrange("p (t n) -> p t n", t=TT), ring[:, 1, 0:D]
            for tt in range(TT):
                link(dve.scalar_tensor_tensor(out_acc[:, tt], out_acc[:, tt], root(4, tt), gf, ALU.mult, ALU.mult))
                dve.tensor_tensor(y_out[:, tt], out_acc[:, tt], res[:, tt], ALU.add).then_inc(fin, 1)

        @block.tensor
        def _(pe):
            pe.wait_ge(con_in, 32)
            pe.wait_ge(rpb_in, 16 * 2 * NA_H)
            back = tab_back[:].rearrange("p h r c -> p (h r c)")
            for i in range(NA_H * 6 * GRID // BANK):
                b = open_bank(pe, "tab", i)
                pe.matmul(b[:], flip[:], back[:, i * BANK:(i + 1) * BANK], start=True, stop=True).then_inc(full_f, 1)

            def mod(v):
                i = (0, 1, *ADA_LATE).index(v)
                pe.wait_ge(ada_used, 4 * i + 4)
                for half in range(2):
                    b = open_bank(pe, "mod", v, half)
                    pe.matmul(b[:], ones, acc[:, i % 2, half * BANK:(half + 1) * BANK], start=True, stop=True).then_inc(full_f, 1)

            def turn_tile(name, src, ready, n):
                for tt in range(TT):
                    pe.wait_ge(ready, n * (tt + 1))
                    for q in range(2):
                        b = open_bank(pe, name, tt, q)
                        for cc in range(4):
                            ins = pe.transpose(b[:, cc * P:(cc + 1) * P], src[:, tt, (4 * q + cc) * P:(4 * q + cc + 1) * P], ident)
                        ins.then_inc(full_f, 1)

            mod(0)
            mod(1)
            turn_tile("hT", h, h_made, 1)
            for tt in range(TT):
                for q in range(2):
                    drained(pe, "hT", tt, q)

            def hidden(tt, k):
                return hT[:, k, tt * P:(tt + 1) * P]

            lat_banks = [[open_bank(pe, "lat", tt, part) for part in range(2)] for tt in range(TT)]
            for u in range(3):
                arrived(pe, "lat", u)
                ks = range(3 * u, min(KD, 3 * u + 3))
                view = unit_at("lat", u)[:, 0:len(ks) * LAT].rearrange("p (k n) -> p k n", k=len(ks))
                for tt in range(TT):
                    for part, (c0, c1) in enumerate(((0, BANK), (BANK, LAT))):
                        for i, k in enumerate(ks):
                            ins = pe.matmul(lat_banks[tt][part][:, 0:c1 - c0], hidden(tt, k), view[:, i, c0:c1], start=(k == 0), stop=(k == KD - 1))
                        if u == 2:
                            ins.then_inc(full_f, 1)
                if u < 2:
                    ins.then_inc(pe_used, 1)
            for name in "qk":
                banks = [open_bank(pe, name, cc) for cc in range(4)]
                for u in range(2):
                    arrived(pe, name, u)
                    view = unit_at(name, u).rearrange("p (k n) -> p k n", k=4)
                    for cc in range(4):
                        for i in range(4):
                            ins = pe.matmul(banks[cc][:, 0:TT * P], view[:, i, cc * P:(cc + 1) * P], hT[:, 4 * u + i, :], start=(u == 0 and i == 0), stop=(u == 1 and i == 3))
                        if u == 1:
                            ins.then_inc(full_f, 1)
                    if u == 0:
                        ins.then_inc(pe_used, 1)

            def two_tiles(name, keys, k_units):
                banks = [open_bank(pe, *key) for key in keys]
                for u in range(k_units):
                    arrived(pe, *name, u)
                    view = unit_at(*name, u).rearrange("p (k n) -> p k n", k=4)
                    for tt in range(TT):
                        for i in range(4):
                            ins = pe.matmul(banks[tt][:], hidden(tt, 4 * u + i), view[:, i], start=(u == 0 and i == 0), stop=(u == 1 and i == 3))
                        if u == k_units - 1:
                            ins.then_inc(full_f, 1)
                    if u < k_units - 1:
                        ins.then_inc(pe_used, 1)

            two_tiles(("v",), [("v", tt) for tt in range(TT)], 2)
            for tt in range(TT):
                pe.wait_ge(lat_made, tt + 1)
                for name, c0, nch in (("cqT", 0, 3), ("ckT", 3, 2)):
                    b = open_bank(pe, name, tt)
                    for cc in range(nch):
                        ins = pe.transpose(b[:, cc * P:(cc + 1) * P], lat[:, tt, (c0 + cc) * P:(c0 + cc + 1) * P], ident)
                    ins.then_inc(full_f, 1)
            for tt in range(TT):
                drained(pe, "cqT", tt)
                drained(pe, "ckT", tt)
            banks = [[open_bank(pe, "uq", tt, half) for half in range(2)] for tt in range(TT)]
            for u in range(2):
                arrived(pe, "uq", u)
                ks = ((0, 1), (2,))[u]
                view = unit_at("uq", u)[:, 0:len(ks) * M_H * QK].rearrange("p (k n) -> p k n", k=len(ks))
                for tt in range(TT):
                    for half in range(2):
                        for i, k in enumerate(ks):
                            ins = pe.matmul(banks[tt][half][:, 0:384], cT[:, k, tt * P:(tt + 1) * P], view[:, i, half * 384:(half + 1) * 384], start=(k == 0), stop=(k == 2))
                        if u == 1:
                            ins.then_inc(full_f, 1)
                if u == 0:
                    ins.then_inc(pe_used, 1)
            arrived(pe, "ukv", 0)
            view = unit_at("ukv", 0).rearrange("p (k n) -> p k n", k=2)
            for tt in range(TT):
                for half in range(2):
                    b = open_bank(pe, "ukv", tt, half)
                    for i in range(2):
                        ins = pe.matmul(b[:], cT[:, 3 + i, tt * P:(tt + 1) * P], view[:, i, half * BANK:(half + 1) * BANK], start=(i == 0), stop=(i == 1))
                    ins.then_inc(full_f, 1)
            for name, src, ready in (("mkT", k96, krope), ("mqT", qm, qrope)):
                for tt in range(TT):
                    pe.wait_ge(ready, tt + 1)
                    if name == "mkT":
                        drained(pe, "ukv", tt, 1)
                    for g in range(2):
                        b = open_bank(pe, name, tt, g)
                        for cc in range(4):
                            hd = 4 * g + cc
                            s = src[:, tt, hd, :] if name == "mkT" else src[:, tt, hd * QK:(hd + 1) * QK]
                            ins = pe.transpose(b[0:QK, cc * P:(cc + 1) * P], s, ident)
                        ins.then_inc(full_f, 1)
            for tt in range(TT):
                drained(pe, "q", 3), drained(pe, "k", 3), drained(pe, "v", tt)

            def scores(n):
                br, tt, hp = n // 8, n // 4 % 2, n % 4
                b = open_bank(pe, "s", n)
                if n == 8:
                    for t in range(TT):
                        drained(pe, "mqT", t, 1), drained(pe, "mkT", t, 1)
                for hh in range(2):
                    if br == 0:
                        lhs = qT[hh * 64:(hh + 1) * 64, hp, tt * P:(tt + 1) * P]
                        rhs = kT[hh * 64:(hh + 1) * 64, hp, :]
                    else:
                        lhs, rhs = mqT[:, 2 * hp + hh, tt * P:(tt + 1) * P], mkT[:, 2 * hp + hh, :]
                    ins = pe.matmul(b[:, hh * 256:(hh + 1) * 256], lhs, rhs, start=True, stop=True)
                    if br == 0 and hh == 0:
                        ins.then_inc(head_scored, 1)
                        pe.wait_ge(head_scored, n + 1)
                ins.then_inc(full_f, 1)

            scores(0)
            scores(1)
            for n in range(16):
                br, tt, hp = n // 8, n // 4 % 2, n % 4
                pe.wait_ge(exps, n + 1)
                b = open_bank(pe, "pT", n)
                for cc in range(4):
                    ins = pe.transpose(b[:, cc * P:(cc + 1) * P], p_sb[:, n % 2, cc // 2, (cc % 2) * P:(cc % 2 + 1) * P], ident)
                ins.then_inc(full_f, 1)
                if n + 2 < 16:
                    scores(n + 2)
                drained(pe, "pT", n)
                o = open_bank(pe, "o", n // 4) if hp == 0 else bank("o", n // 4)
                vv = v_m if br else v_na
                for hh in range(2):
                    hd = 2 * hp + hh
                    for kc in range(2):
                        ins = pe.matmul(o[:, hd * 64:(hd + 1) * 64], pT[:, n % 2, 2 * hh + kc], vv[:, kc, hd * 64:(hd + 1) * 64], start=(kc == 0), stop=(kc == 1))
                ins.then_inc(pv, 1)
                if n % 4 == 2:
                    two_tiles(("gate", n // 4), [("gate", n // 4, t) for t in range(TT)], 2)
                if n in MOD_AFTER:
                    mod(MOD_AFTER[n])
            for a in range(4):
                drained(pe, "o", a)
                b = open_bank(pe, "oT", a)
                for cc in range(4):
                    ins = pe.transpose(b[:, cc * P:(cc + 1) * P], o_sb[:, a, cc * P:(cc + 1) * P], ident)
                ins.then_inc(full_f, 1)
            for br in range(2):
                for tt in range(TT):
                    drained(pe, "oT", 2 * br + tt)
                banks = [[open_bank(pe, "up", br, tt, half) for half in range(2)] for tt in range(TT)]
                for u in range(2):
                    arrived(pe, "up", br, u)
                    view = unit_at("up", br, u).rearrange("p (k n) -> p k n", k=2)
                    for tt in range(TT):
                        for half in range(2):
                            for i in range(2):
                                ins = pe.matmul(banks[tt][half][:], oT[:, 4 * br + 2 * u + i, tt * P:(tt + 1) * P], view[:, i, half * BANK:(half + 1) * BANK], start=(u == 0 and i == 0), stop=(u == 1 and i == 1))
                            if u == 1:
                                ins.then_inc(full_f, 1)
                    if u == 0:
                        ins.then_inc(pe_used, 1)
            turn_tile("mT", h, merged_s, 2)
            for tt in range(TT):
                for q in range(2):
                    drained(pe, "mT", tt, q)
            banks = [[open_bank(pe, "y", tt, half) for half in range(2)] for tt in range(TT)]
            for u in range(4):
                arrived(pe, "out", u)
                view = unit_at("out", u).rearrange("p (k n) -> p k n", k=2)
                for tt in range(TT):
                    for half in range(2):
                        for i in range(2):
                            ins = pe.matmul(banks[tt][half][:], hidden(tt, 2 * u + i), view[:, i, half * BANK:(half + 1) * BANK], start=(u == 0 and i == 0), stop=(u == 3 and i == 1))
                        if u == 3:
                            ins.then_inc(full_f, 1)
                if u < 3:
                    ins.then_inc(pe_used, 1)
            turn_tile("h2T", h, h2_made, 1)
            pe.wait_ge(router_in, 32)
            for tt in range(TT):
                for q in range(2):
                    drained(pe, "h2T", tt, q)
                b = open_bank(pe, "lg", tt)
                for k in range(KD):
                    ins = pe.matmul(b[:, 0:NE], hidden(tt, k), wr[:, k], start=(k == 0), stop=(k == KD - 1))
                ins.then_inc(full_f, 1)
            MASK, GATE = 10, 12
            for tt in range(TT):
                pe.wait_ge(mask_made, tt + 1)
                b = open_bank(pe, "pos", tt)
                if tt:
                    pe.matmul(b[:, 0:NE], ones, rt[:, MASK], start=True, stop=False)
                pe.matmul(b[:, 0:NE], tri, rt[:, MASK + tt], start=(tt == 0), stop=True).then_inc(full_f, 1)
            b = open_bank(pe, "cnt")
            for tt in range(TT):
                ins = pe.matmul(b[:, 0:NE], ones, rt[:, MASK + tt], start=(tt == 0), stop=(tt == 1))
            ins.then_inc(full_f, 1)
            for tt in range(TT):
                pe.wait_ge(gate_made, tt + 1)
                b = open_bank(pe, "gT", tt)
                pe.transpose(b[0:NE, 0:P], rt[:, GATE + tt], ident).then_inc(full_f, 1)
            pe.wait_ge(b2_in, 16)
            for tt in range(TT):
                drained(pe, "gT", tt)
                for half in range(2):
                    b = open_bank(pe, "b2", tt, half)
                    pe.matmul(b[:], gT[:, tt * P:(tt + 1) * P], b2sb[:, half * BANK:(half + 1) * BANK], start=True, stop=True).then_inc(full_f, 1)
            pe.wait_ge(out_act, front_drains["act"])
            pe.wait_ge(out_dve, front_drains["dve"])
            pe.wait_ge(xhi_made, 2)
            pe.wait_ge(xlo_made, 2)
            pe.wait_ge(tabs_made, 1)

            def free(count, r):
                by_act, n = count
                pe.wait_ge(drain_act if by_act else drain_dve, n + r * (ACT_DRAINS if by_act else DVE_DRAINS))

            def gather_fill(q, target):
                for cc in range(4):
                    k = 4 * (q % 2) + cc
                    dst = target[:, cc * P:(cc + 1) * P]
                    for tt in range(TT):
                        src = xs_hi if q < 2 else xs_lo
                        ins = pe.matmul(dst, src[:, tt, k], sel_t[:, tt], start=(tt == 0), stop=(tt == 1 and q >= 2), skip_group_check=True)
                    if q < 2:
                        for tt in range(TT):
                            ins = pe.matmul(dst[:, HALF:P], xs_lo[:, tt, k], sela_t[:, tt, HALF:P], start=False, stop=(tt == 1), skip_group_check=True)
                ins.then_inc(misc_full, 1)

            def sweep(r):
                def flag(e):
                    if r:
                        return None
                    return pe.value_load(cnt_i[0:1, e:e + 1] if isinstance(e, int) else cnt_i[0:1, bass.ds(e, 1)], min_val=0, max_val=TT * P)

                def many(count, body):
                    if count is None:
                        body()
                    else:
                        with pe.If(count > half_cap):
                            body()

                def w1_unit(m_no, q, k, par, count, lo_wait):
                    pe.wait_ge(hi_ready, r * UNITS + m_no + 1)
                    for n4 in range(4):
                        pe.matmul(ps[n4][:], t1[:, par, k], whi[:, q, n4 * BANK:(n4 + 1) * BANK], start=(k == 0), stop=False, skip_group_check=True)
                    wait_lo(pe, lo_wait, r)

                    def lo_tokens():
                        for w in (whi, wlo):
                            for n4 in range(4):
                                pe.matmul(ps[n4][:], t2[:, par, k], w[:, q, n4 * BANK:(n4 + 1) * BANK], start=False, stop=False, skip_group_check=True)

                    many(count, lo_tokens)
                    for n4 in range(4):
                        ins = pe.matmul(ps[n4][:], t1[:, par, k], wlo[:, q, n4 * BANK:(n4 + 1) * BANK], start=False, stop=(k == KD - 1), skip_group_check=True)
                    ins.then_inc(split_used, 1)

                for par in range(2):
                    pe.wait_ge(sel_made, r * NE + par + 1)
                    for q in range(4):
                        f = 4 * par + q
                        if f >= 2:
                            pe.wait_ge(drain_act, r * ACT_DRAINS + f - 1)
                        elif r:
                            pe.wait_ge(drain_dve, r * DVE_DRAINS - 1 + f)
                        gather_fill(q, ps[6 + f % 2])
                pe.wait_ge(drain_act, r * ACT_DRAINS + 4)
                count = flag(0)
                for m in range(4):
                    w1_unit(m, m % SPLITS, m, 0, count, lo_count_of_unit(m))

                def step(e, b):
                    par = (e if isinstance(e, int) else b) % 2
                    count = flag(e)
                    following = None if last(e) else flag(e + 1)
                    for j in range(4):
                        w1_unit(unit_no(e, j), split_slot(e, j), 4 + j, par, count, lo_count(e, j))
                    if not no_gather(e):
                        pe.wait_ge(sel_made, r * NE + e + 3)
                        for q in range(4):
                            kind = "g%d" % q
                            free(two_before(e, kind), r)
                            gather_fill(q, ps[6 + bank_of(e, kind, b)])
                    pe.wait_ge(hs_act, r * NE + e + 1)
                    pe.wait_ge(hs_dve, r * NE + e + 1)
                    pe.wait_ge(fold_made, r * NE + e + 1)
                    turned = hs[:].rearrange("s (p k g) -> s g k p", k=KD, g=2)
                    for f in range(4):
                        kind = "f%d" % f
                        free(two_before(e, kind), r)
                        dst = ps[6 + bank_of(e, kind, b)]
                        for g in range(2):
                            for kk in range(2):
                                cc = 2 * g + kk
                                ins = pe.matmul(dst[:, cc * P:(cc + 1) * P], turned[:, g, 2 * f + kk, :], fmat[:], start=True, stop=True)
                        ins.then_inc(misc_full, 1)
                    if not last(e):
                        if isinstance(e, int) and e == 0:
                            pe.wait_ge(drain_act, r * ACT_DRAINS + PRE_FILLS)
                        else:
                            pe.wait_ge(drain_act, r * ACT_DRAINS + drains(e - 1, "g3")[1])
                        for j in range(4, 8):
                            w1_unit(unit_no(e, j), split_slot(e, j), j - 4, 1 - par, following, lo_count(e, j))
                    pe.wait_ge(w_made, r * NE + e + 1)
                    free(two_before(e, "w"), r)
                    dst = ps[6 + bank_of(e, "w", b)]
                    for tt in range(TT):
                        ins = pe.transpose(dst[:, tt * P:(tt + 1) * P], wsel[:, tt], ident)
                    ins.then_inc(misc_full, 1)
                    pe.wait_ge(u_ready, r * NE + e + 1)
                    if not (isinstance(e, int) and e == 0 and r == 0):
                        pe.wait_ge(ys_made, r * NE + e)
                    for j in range(8, 12):
                        q = split_slot(e, j)
                        hi_v = whi[:, q].rearrange("p (k n) -> p k n", k=2)
                        lo_v = wlo[:, q].rearrange("p (k n) -> p k n", k=2)
                        pe.wait_ge(hi_ready, r * UNITS + unit_no(e, j) + 1)

                        def products(u, w, starts, stops):
                            for i in range(2):
                                kk = 2 * (j - 8) + i
                                for half in range(2):
                                    ins = pe.matmul(ps[4 + half][:], u[:, kk], w[:, i, half * BANK:(half + 1) * BANK],
                                                    start=(starts and kk == 0), stop=(stops and kk == KD - 1), skip_group_check=True)
                            return ins

                        products(u1, hi_v, True, False)
                        wait_lo(pe, lo_count(e, j), r)

                        def lo_slots():
                            products(u2, hi_v, False, False)
                            products(u2, lo_v, False, False)

                        many(count, lo_slots)
                        products(u1, lo_v, False, True).then_inc(split_used, 1)
                    pe.wait_ge(ys_made, r * NE + e + 1)
                    for q in range(4):
                        kind = "c%d" % q
                        free(two_before(e, kind), r)
                        if q == 0:
                            free(drains(e, "w"), r)
                        pe.matmul(ps[6 + bank_of(e, kind, b)][:], wT[:, (q // 2) * P:(q // 2 + 1) * P], ys[:, (q % 2) * BANK:(q % 2 + 1) * BANK],
                                  start=True, stop=True).then_inc(misc_full, 1)

                over_experts(pe, step)

            two_sweeps(pe, sweep)


_INS = ["x", "c", "w_ada", "b_ada", "g_attn_pre", "g_attn_post", "w_in", "b_gate", "na_rpb", "q_norm_g", "kv_norm_g",
        "w_uq", "w_ukv", "w_na_up", "w_mla_up", "w_out", "g_ffn_pre", "g_ffn_post", "w_router", "b_router",
        "w1", "b1", "w2", "b2"]


def constants():
    import numpy as np

    p, j = np.arange(P)[:, None], np.arange(P)[None, :]
    con = np.zeros((P, C_WIDTH), np.float32)
    con[:, C_ID:C_ID + P] = p == j
    con[:, C_TRI:C_TRI + P] = p < j
    con[:, C_ONE:C_ONE + P] = 1
    con[:, C_J:C_J + P] = j
    con[:, C_JM:C_JM + P] = j % HALF
    con[:, C_OFF:C_OFF + P] = abs(p - j) == HALF
    con[:, C_FLIP:C_FLIP + P] = (p // GRID == j // GRID) & (p % GRID == GRID - 1 - j % GRID)
    qc, kc = np.arange(P)[:, None] % GRID, np.arange(GRID)[None, :]
    first = np.clip(qc - 8, 0, GRID - 16)
    con[:, C_MASK:C_MASK + GRID] = np.where((kc >= first) & (kc < first + 16), 0, -1e30)
    nf = ROPE // 4
    inv = np.float32(100.0) ** (-np.arange(nf, dtype=np.float32) / np.float32(nf))
    for tt in range(TT):
        t = tt * P + np.arange(P)
        for a, position in enumerate((t // GRID, t % GRID)):
            angle = position.astype(np.float32)[:, None] * inv
            o = 16 * tt + 8 * a
            con[:, C_COS + o:C_COS + o + 8] = np.cos(angle)
            con[:, C_SIN + o:C_SIN + o + 8] = np.sin(angle)
    return con


def kernel(**inputs):
    import numpy as np
    import concourse.bacc as bacc
    from concourse.bass_utils import run_bass_kernel_spmd

    nc = bacc.Bacc("TRN2", target_bir_lowering=False, num_devices=1)
    arrays, args = {}, []
    for name in _INS:
        a = np.ascontiguousarray(inputs[name])
        arrays[f"in_{name}"] = a
        args.append(nc.dram_tensor(f"in_{name}", a.shape, mybir.dt.from_np(a.dtype), kind="ExternalInput").ap())
    arrays["in_consts"] = constants()
    args.append(nc.dram_tensor("in_consts", (P, C_WIDTH), F32, kind="ExternalInput").ap())
    args.append(nc.dram_tensor("out_x", (1, TT * P, D), F32, kind="ExternalOutput").ap())
    build(nc, *args)
    r = run_bass_kernel_spmd(nc, [arrays], core_ids=[0])
    return r.results[0]["out_x"]
```

```python
from contextlib import ExitStack

import concourse.bass as bass
from concourse import mybir

F32 = mybir.dt.float32
F32R = mybir.dt.float32r
I32 = mybir.dt.int32
U32 = mybir.dt.uint32
ALU = mybir.AluOpType
ACT = mybir.ActivationFunctionType
AX = mybir.AxisListType.X

P = 128
TT = 2
D = 1024
KD = D // P
BANK = 512
UNIT = 2048
SLOTS = 8
SPLITS = 6
GRID = 64
NA_H, NA_D, NA_W = 8, 64, 512
RPB_R, RPB_C = 15, 31
M_H, NOPE, ROPE, QK = 8, 64, 32, 96
Q_LORA, KV_LORA = 384, 256
LAT = Q_LORA + KV_LORA + ROPE
NE, TOPK = 32, 4
EPS = 1e-6
HALF = P // 2
ALPHA, LIMIT = 1.702, 7.0
FULL = P

C_ID, C_TRI, C_ONE, C_J, C_JM, C_OFF, C_MASK, C_COS, C_SIN = 0, 128, 256, 384, 512, 640, 768, 832, 864
C_ALL = 896
C_FLIP = 896
C_WIDTH = 1024

K = 1024
A_X, A_MOD, A_GBC, A_H, A_HT, A_QKT, A_V, A_G2, A_G3, A_VM, A_MQK, A_GATE, A_TAB, A_ADA, A_END = (
    0, 8 * K, 24 * K, 32 * K, 40 * K, 48 * K, 56 * K, 60 * K, 72 * K, 80 * K, 84 * K, 100 * K, 116 * K,
    128 * K, 136 * K)


def front_jobs():
    jobs = []

    def job(eng, *key):
        jobs.append((key, eng))

    def mod(v):
        for half in range(2):
            job("act" if v in (0, 3) else "dve", "mod", v, half)

    mod(0), mod(1)
    for tt in range(TT):
        for q in range(2):
            job("dve" if q else "act", "hT", tt, q)
    for tt in range(TT):
        for part in range(2):
            job("act" if part else "dve", "lat", tt, part)
    for i in range(NA_H * 6 * GRID // BANK):
        job("dve", "tab", i)
    for name in "qk":
        for c in range(4):
            job("act", name, c)
    for tt in range(TT):
        job("dve", "v", tt)
    for tt in range(TT):
        job("dve", "cqT", tt)
        job("act", "ckT", tt)
    for tt in range(TT):
        for half in range(2):
            job("dve", "uq", tt, half)
    for tt in range(TT):
        for half in range(2):
            job("act", "ukv", tt, half)
    for tt in range(TT):
        for g in range(2):
            job("dve", "mkT", tt, g)
    for tt in range(TT):
        for g in range(2):
            job("act", "mqT", tt, g)
    job("dve", "s", 0)
    job("dve", "s", 1)
    for n in range(16):
        job("act", "pT", n)
        if n + 2 < 16:
            job("dve", "s", n + 2)
        if n % 4 == 3:
            job("dve", "o", n // 4)
        if n % 4 == 2:
            for tt in range(TT):
                job("dve", "gate", n // 4, tt)
        if n in MOD_AFTER:
            mod(MOD_AFTER[n])
    for a in range(4):
        job("dve" if a % 2 else "act", "oT", a)
    for br in range(2):
        for tt in range(TT):
            for half in range(2):
                job("dve", "up", br, tt, half)
    for tt in range(TT):
        for q in range(2):
            job("dve" if q else "act", "mT", tt, q)
    for tt in range(TT):
        for half in range(2):
            job("act", "y", tt, half)
    for tt in range(TT):
        for q in range(2):
            job("dve" if q else "act", "h2T", tt, q)
    for tt in range(TT):
        job("dve", "lg", tt)
    for tt in range(TT):
        job("dve", "pos", tt)
    job("dve", "cnt")
    for tt in range(TT):
        job("dve", "gT", tt)
    for tt in range(TT):
        for half in range(2):
            job("act", "b2", tt, half)
    return jobs


ADA_LATE = (2, 4, 3, 5)
MOD_AFTER = {4: 2, 8: 4, 12: 3, 15: 5}


def front_units():
    units = [("ada", v, u, "dve") for v in (0, 1) for u in range(4)]
    units += [("lat", u, "pe") for u in range(2)] + [("lat", 2, ("lat", 1, 1))]
    units += [(n, u, ("pe", (n, 3))[u]) for n in "qk" for u in range(2)]
    units += [("v", u, ("pe", ("v", 1))[u]) for u in range(2)]
    units += [("uq", u, ("pe", ("uq", 1, 1))[u]) for u in range(2)] + [("ukv", 0, ("ukv", 1, 1))]
    for n in range(16):
        units.append(("ada", ADA_LATE[n // 4], n % 4, "dve"))
        if n % 4 == 2:
            units += [("gate", n // 4, u, ("pe", ("gate", n // 4, 1))[u]) for u in range(2)]
    units += [("up", br, u, ("pe", ("up", br, 1, 1))[u]) for br in range(2) for u in range(2)]
    units += [("out", u, ("pe", ("y", 1, 1))[u == 3]) for u in range(4)]
    return units


UNITS = 12 * NE
FILLS = 9 * NE
DVE_DRAINS = 8 * NE
AHEAD = 3


def last(e):
    return isinstance(e, int) and e == NE - 1


def no_gather(e):
    return isinstance(e, int) and e >= NE - 2


def unit_no(e, j):
    return 8 + 12 * e + j - (8 if last(e) else 0)


def step_units(e):
    return list(range(8, 12) if last(e) else range(12))


def split_slot(e, j):
    return unit_no(e, j) % SPLITS if isinstance(e, int) else (8 + j) % SPLITS


def ring_slot(e, b, j, base):
    return (base + unit_no(e, j)) % SLOTS if isinstance(e, int) else (base + 8 + 12 * b + j) % SLOTS


def by_pool(e, j):
    return unit_no(e, j) % 3 == 0 if isinstance(e, int) else (8 + j) % 3 == 0


def lo_units(e, pool):
    return [j for j in step_units(e) if by_pool(e, j) == pool]


def lo_count(e, j):
    if isinstance(e, int):
        return lo_count_of_unit(unit_no(e, j))
    return (True, 4 * e + (8 + j) // 3 + 1) if by_pool(e, j) else (False, 8 * e + (8 + j) - (8 + j) // 3)


def lo_count_of_unit(m):
    return (True, m // 3 + 1) if m % 3 == 0 else (False, m - m // 3)


def sequence(e):
    f, c = ["f0", "f1", "f2", "f3"], ["c0", "c1", "c2", "c3"]
    if isinstance(e, int) and e in (0, NE):
        return f if e == 0 else ["w"] + c
    return ["w"] + f + c


def first_step(e):
    return isinstance(e, int) and e == 0


def fill_no(e, kind):
    return (0 if first_step(e) else 9 * e - 5) + sequence(e).index(kind)


def bank_of(e, kind, b):
    return fill_no(e, kind) % 2 if isinstance(e, int) else (b + 1 + sequence(e).index(kind)) % 2


def drains(e, kind):
    if kind == "w":
        return True, e
    q = [k for k in sequence(e) if k != "w"].index(kind)
    return False, (0 if first_step(e) else 8 * e - 4) + q + 1


def two_before(e, kind):
    q = sequence(e).index(kind)
    if q >= 2:
        return drains(e, sequence(e)[q - 2])
    if first_step(e):
        return None
    return drains(e - 1, sequence(e - 1 if isinstance(e, int) else e)[q - 2])


def build(nc, x, c, w_ada, b_ada, g_attn_pre, g_attn_post, w_in, b_gate, na_rpb, q_norm_g, kv_norm_g,
          w_uq, w_ukv, w_na_up, w_mla_up, w_out, g_ffn_pre, g_ffn_post, w_router, b_router,
          w1, b1, w2, b2, consts, out, full=FULL, half_cap=HALF):
    units = front_units()
    jobs = front_jobs()
    NF = len(units)
    assert (UNITS % SLOTS, UNITS % SPLITS) == (0, 0)

    table, seen, turn, fills = {}, {"act": 0, "dve": 0}, 0, 0
    bank_last = {}
    for key, eng in jobs:
        seen[eng] += 1
        if key[0] == "o":
            bank = 6 + key[1] % 2
        else:
            bank, turn = turn % 6, turn + 1
        fills += key[0] != "o"
        table[key] = (fills, bank, bank_last.get(bank), eng, seen[eng])
        bank_last[bank] = key
    front_drains = dict(seen)

    with ExitStack() as ctx:
        def tile(name, shape, dt=F32):
            return ctx.enter_context(nc.sbuf_tensor("t_" + name, shape, dt))

        def sem(name):
            return ctx.enter_context(nc.semaphore(name))

        ring_off = -(-nc.sbuf_base // 64) * 64
        ring = tile("ring", [P, SLOTS, UNIT])
        ring_lo = nc.alloc_sbuf_tensor_at("t_ring_lo", [P, SLOTS, UNIT], F32R, offset=ring_off)
        con = tile("con", [P, C_ALL])
        b1t = tile("b1t", [P, NE, 16])
        ptab = tile("ptab", [P, NE + 2, 10])
        cnt_i = tile("cnt_i", [P, NE], I32)
        ovf_i = tile("ovf_i", [P, 1], I32)
        st = tile("st", [P, 96])
        mx = tile("mx", [P, 2, 2])
        nmx = tile("nmx", [P, 2, 2])
        lsum = tile("lsum", [P, 32])
        linv = tile("linv", [P, 32])
        lo_off = -(-nc.sbuf_base // 64) * 64
        tile("arena", [P, (A_END + 64) // 4])

        def at(name, off, shape, dt=F32):
            return nc.alloc_sbuf_tensor_at("a_" + name, shape, dt, offset=lo_off + off)

        ident, tri, ones = (con[:, o:o + P] for o in (C_ID, C_TRI, C_ONE))
        iota, iota_mod, offdiag = (con[:, o:o + P] for o in (C_J, C_JM, C_OFF))

        xt = at("x", A_X, [P, TT, D])
        modv = at("mod", A_MOD, [P, 4, D])
        MODV = {0: 0, 1: 1, 2: 2, 4: 3, 3: 0, 5: 1}
        gbc = at("gbc", A_GBC, [P, 2, D])
        h = at("h", A_H, [P, TT, D])
        qm = at("qm", A_H, [P, TT, M_H * QK])
        hT = at("hT", A_HT, [P, KD, TT * P])
        qT = at("qT", A_QKT, [P, 4, TT * P])
        kT = at("kT", A_QKT + 4 * K, [P, 4, TT * P])
        ysb = at("ysb", A_QKT, [P, TT, D])
        v_na = at("v_na", A_V, [P, TT, NA_W])
        lat = at("lat", A_G2, [P, TT, LAT])
        cT = at("cT", A_G2 + 5632, [P, 5, TT * P])
        s_sb = at("s_sb", A_G2, [P, 2, 2, 256])
        p_sb = at("p_sb", A_G2 + 4 * K, [P, 2, 2, 256])
        pT = at("pT", A_G2 + 8 * K, [P, 2, 4, P])
        k96 = at("k96", A_G3, [P, TT, M_H, QK])
        nbc = at("nbc", A_MQK, [P, Q_LORA + KV_LORA])
        o_sb = at("o_sb", A_G3, [P, 4, NA_W])
        v_m = at("v_m", A_VM, [P, TT, NA_W])
        mqT = at("mqT", A_MQK, [QK, M_H, TT * P])
        mkT = at("mkT", A_MQK + 8 * K, [QK, M_H, TT * P])
        oT = at("oT", A_MQK, [P, 8, TT * P])
        gates = at("gates", A_GATE, [P, TT, 2 * D])
        tab = at("tab", A_TAB, [P, NA_H, 6, GRID])
        acc = at("acc", A_ADA, [P, 2, D])
        tab_back = at("tab_back", A_G3, [P, NA_H, 6, GRID])
        flip = at("flip", A_MQK + 4 * K, [P, P])
        rope_s = at("rope_s", A_H + 6 * K, [P, 4, 128])
        wr = at("wr", A_TAB, [P, KD, NE])
        brc = at("brc", A_TAB + K, [P, NE])
        rt = at("rt", A_TAB + K + 128, [P, 16, NE])
        m8 = at("m8", A_TAB + 3 * K + 256, [P, TT, 8])
        gT = at("gT", A_TAB + 3 * K + 512, [NE, TT * P])
        b2sb = at("b2sb", A_G2, [NE, D])

        whi = at("whi", 0, [P, SPLITS, UNIT], F32R)
        hs = at("hs", 48 * K, [P, UNIT])
        hb = at("hb", 56 * K, [P, 4, 2, 2 * P])
        sg = at("sg", 64 * K, [P, 4, 2 * P])
        u1 = at("u1", 68 * K, [P, KD, P], F32R)
        u2 = at("u2", 72 * K, [P, KD, P], F32R)
        ys = at("ys", 76 * K, [P, D])
        scS = at("scS", 80 * K, [P, 10])
        scW = at("scW", 80 * K + 64, [P, 10])
        b1c = at("b1c", 80 * K + 128, [P, 16])
        sel_t = at("sel_t", 80 * K + 512, [P, TT, P], F32R)
        sela_t = at("sela_t", 81 * K + 512, [P, TT, P], F32R)
        wsel = at("wsel", 82 * K + 512, [P, TT, P])
        fmat = at("fmat", 83 * K + 512, [P, P])
        tmpP = at("tmpP", 126 * K + 512, [P, P])
        t1 = at("t1", 84 * K, [P, 2, KD, P], F32R)
        t2 = at("t2", 92 * K, [P, 2, KD, P], F32R)
        xs_hi = at("xs_hi", A_GATE, [P, TT, KD, P], F32R)
        xs_lo = at("xs_lo", A_GATE + 8 * K, [P, TT, KD, P], F32R)
        wT = at("wT", 127 * K, [P, TT * P])
        out_acc = at("out_acc", A_ADA, [P, TT, D])
        res = at("res", 84 * K, [P, TT, D])
        gf = at("gf", 92 * K, [P, D])
        y_out = at("y_out", 0, [P, TT, D])

        ps = [ctx.enter_context(nc.psum_tensor(f"bank{i}", [P, BANK], F32)) for i in range(8)]

        saved_x = nc.dram_tensor("saved_x", [P, TT, D], F32, kind="Internal").ap()
        saved_g = nc.dram_tensor("saved_g", [P, D], F32, kind="Internal").ap()

        landed = [sem(f"landed{i}") for i in range(SLOTS)]
        x_in, c_in, con_in, rpb_in, nbc_in = (sem(n) for n in ("x_in", "c_in", "con_in", "rpb_in", "nbc_in"))
        gain_pre_in, gain_post_in = sem("gain_pre_in"), sem("gain_post_in")
        bgate_in, b1_in, router_in, b2_in = (sem(n) for n in ("bgate_in", "b1_in", "router_in", "b2_in"))
        ada_row = [sem(f"ada_row{i}") for i in range(2)]
        x_saved, g_saved, back_in, stored = (sem(n) for n in ("x_saved", "g_saved", "back_in", "stored"))
        full_f, out_act, out_dve = sem("front_full"), sem("front_act"), sem("front_dve")
        pe_used, ada_used, head_scored = sem("pe_used"), sem("ada_used"), sem("head_scored")
        acc_clear, acc_made = sem("acc_clear"), sem("acc_made")
        csig, sc_made, ms, var, rstd = (sem(n) for n in ("csig", "sc_made", "ms", "var", "rstd"))
        lat_made, krope, qrope, dve_q = (sem(n) for n in ("lat_made", "krope", "qrope", "dve_q"))
        pool_q, h_made, negmax, exps, pv = (sem(n) for n in ("pool_q", "h_made", "negmax", "exps", "pv"))
        sig_made, merged_s, x1_made, h2_made, xhi_made, xlo_made = (
            sem(n) for n in ("sig_made", "merged", "x1_made", "h2_made", "xhi_made", "xlo_made"))
        nv1, ex_made, mask_made, gate_made, tabs_made, fin = (
            sem(n) for n in ("nv1", "ex_made", "mask_made", "gate_made", "tabs_made", "fin"))
        hi_ready, lo_dve, lo_pool, split_used = (sem(n) for n in ("hi_ready", "lo_dve", "lo_pool", "split_used"))
        misc_full, drain_act, drain_dve = sem("misc_full"), sem("drain_act"), sem("drain_dve")
        hs_act, hs_dve, sel_made, w_made, fold_made, par_made = (
            sem(n) for n in ("hs_act", "hs_dve", "sel_made", "w_made", "fold_made", "par_made"))
        glu_made, lin_made, sg_made, a1_made, a_made, u1_made, u2_made, u_ready, ys_made = (
            sem(n) for n in ("glu_made", "lin_made", "sg_made", "a1_made", "a_made", "u1_made", "u2_made", "u_ready", "ys_made"))
        gather_full, gather_used = sem("gather_full"), sem("gather_used")
        pool_m, gates_joined, picked = sem("pool_m"), sem("gates_joined"), sem("picked")

        def unit_index(*name):
            return next(n for n, u in enumerate(units) if u[:-1] == name)

        def unit_at(*name):
            return ring[:, unit_index(*name) % SLOTS, :]

        def arrived(eng, *name):
            n = unit_index(*name)
            eng.wait_ge(landed[n % SLOTS], 16 * (n // SLOTS + 1))

        def filled(eng, *key):
            if key[0] == "o":
                eng.wait_ge(pv, 4 * key[1] + 4)
            else:
                eng.wait_ge(full_f, table[key][0])

        def drained(eng, *key):
            _, _, _, who, count = table[key]
            eng.wait_ge(out_act if who == "act" else out_dve, count)

        def bank(*key):
            return ps[table[key][1]]

        def open_bank(pe, *key):
            before = table[key][2]
            if before is not None:
                drained(pe, *before)
            return bank(*key)

        order = {"act": [k for k, g in jobs if g == "act"], "dve": [k for k, g in jobs if g == "dve"]}

        def take(eng, who, *key):
            assert order[who].pop(0) == key, key
            filled(eng, *key)
            return bank(*key)

        def front_source(name):
            n = name[0]
            if n == "ada":
                _, v, u, _ = name
                s = w_ada[0].rearrange("(p k) n -> p k n", k=KD)[:, 2 * u:2 * u + 2, v * D:(v + 1) * D]
                return s, 2, D
            if n in ("q", "k", "v", "gate"):
                u = name[-2]
                c0 = {"q": 0, "k": NA_W, "v": 2 * NA_W}.get(n)
                if n == "gate":
                    c0 = 3 * NA_W + LAT + name[1] * BANK
                return w_in[0].rearrange("(k p) n -> p k n", p=P)[:, 4 * u:4 * u + 4, c0:c0 + BANK], 4, BANK
            if n == "lat":
                k0, k1 = 3 * name[1], min(KD, 3 * name[1] + 3)
                c0 = 3 * NA_W
                return w_in[0].rearrange("(k p) n -> p k n", p=P)[:, k0:k1, c0:c0 + LAT], k1 - k0, LAT
            if n == "uq":
                k0, k1 = (0, 2) if name[1] == 0 else (2, 3)
                return w_uq[0].rearrange("(k p) h d -> p k (h d)", p=P)[:, k0:k1], k1 - k0, M_H * QK
            if n == "ukv":
                return w_ukv[0].rearrange("(k p) h d -> p k (h d)", p=P), 2, D
            if n == "up":
                w = (w_na_up, w_mla_up)[name[1]]
                return w[0].rearrange("(k p) n -> p k n", p=P)[:, 2 * name[2]:2 * name[2] + 2], 2, D
            return w_out[0].rearrange("(k p) n -> p k n", p=P)[:, 2 * name[1]:2 * name[1] + 2], 2, D

        def wait_lo(eng, count, r):
            pools, n = count
            eng.wait_ge(lo_pool if pools else lo_dve, n + r * (UNITS // 3 if pools else 2 * UNITS // 3))

        def over_experts(eng, step):
            step(0, 0)
            step(1, 1)
            with eng.Fori(1, NE // 2 - 1) as i:
                step(2 * i, 0)
                step(2 * i + 1, 1)
            step(NE - 2, 0)
            step(NE - 1, 1)

        def two_sweeps(eng, sweep, between=None, after=None):
            sweep(0)
            eng.wait_ge(tabs_made, 1)
            more = eng.value_load(ovf_i[0:1, 0:1], min_val=0, max_val=TT * P)
            with eng.If(more > full):
                if between:
                    between()
                sweep(1)
                if after:
                    after()
                eng.drain()

        def over_experts_i(eng, step, pair_of):
            step(0, 0)
            step(1, 1)
            with eng.Fori(1, NE // 2 - 1) as i:
                pair_of["i"] = i
                step(2 * i, 0)
                step(2 * i + 1, 1)
            pair_of["i"] = None
            step(NE - 2, 0)
            step(NE - 1, 1)

        block = ctx.enter_context(nc.Block())

        @block.sync
        def _(sp):
            sp.dma_start(st[:, 0:8], c[0].rearrange("(p k) -> p k", k=KD)).then_inc(c_in, 16)
            sp.dma_start(xt[:], x[0].rearrange("(t p) n -> p t n", p=P)).then_inc(x_in, 16)
            sp.dma_start(con[:], consts[:, 0:C_ALL]).then_inc(con_in, 16)
            sp.dma_start(flip[:], consts[:, C_FLIP:C_FLIP + P]).then_inc(con_in, 16)

            def read_before(n):
                who = units[n][-1]
                if who in ("dve", "pe"):
                    sp.wait_ge(ada_used if who == "dve" else pe_used, sum(u[-1] == who for u in units[:n + 1]))
                else:
                    filled(sp, *who)

            for n, name in enumerate(units):
                if n >= SLOTS:
                    read_before(n - SLOTS)
                src, k, cols = front_source(name)
                dst = ring[:, n % SLOTS, 0:k * cols].rearrange("p (k n) -> p k n", k=k)
                sp.dma_start(dst, src).then_inc(landed[n % SLOTS], 16)

            w1_v = w1[0].rearrange("e (p k) n -> e p k n", k=KD)
            w2_v = w2[0].rearrange("e (p k) n -> e p k n", k=KD)

            def w1_unit(e, k, slot):
                sp.dma_start(ring[:, slot, :], w1_v[e, :, k, :]).then_inc(landed[slot], 16)

            def load(e, b, j):
                slot = ring_slot(e, b, j, NF)
                if j < 8:
                    w1_unit(e + 1, j, slot)
                else:
                    sp.dma_start(ring[:, slot, :].rearrange("p (k n) -> p k n", k=2),
                                 w2_v[e, :, 2 * (j - 8):2 * (j - 8) + 2, :]).then_inc(landed[slot], 16)

            def sweep(r):
                for m in range(8):
                    if r:
                        sp.wait_ge(split_used, r * UNITS + m + 1 - SLOTS)
                    else:
                        read_before(NF + m - SLOTS)
                    w1_unit(0, m, (NF + m) % SLOTS)

                def step(e, b):
                    for j in step_units(e):
                        sp.wait_ge(split_used, r * UNITS + unit_no(e, j) + 1 - SLOTS)
                        load(e, b, j)

                over_experts(sp, step)

            two_sweeps(sp, sweep, after=lambda: sp.wait_ge(split_used, 2 * UNITS))
            sp.wait_ge(split_used, UNITS - 4)
            sp.wait_ge(x_saved, 16)
            sp.wait_ge(g_saved, 16)
            sp.dma_start(res[:], saved_x).then_inc(back_in, 16)
            sp.dma_start(gf[:], saved_g).then_inc(back_in, 16)
            for tt in range(TT):
                sp.wait_ge(fin, tt + 1)
                sp.dma_start(out[0, tt * P:(tt + 1) * P, :], y_out[:, tt, :]).then_inc(stored, 16)
            sp.wait_ge(stored, 16 * TT)

        @block.gpsimd
        def _(pool):
            def start_acc(i):
                v = (0, 1, *ADA_LATE)[i]
                if i >= 2:
                    filled(pool, "mod", (0, 1, *ADA_LATE)[i - 2], 1)
                pool.memset(acc[:, i % 2, :], 0.0).then_inc(acc_clear, 1)
                pool.wait_ge(acc_clear, i + 1)
                pool.dma_start(acc[0:1, i % 2, :], b_ada[:, v * D:(v + 1) * D]).then_inc(ada_row[i % 2], 16)

            start_acc(0)
            start_acc(1)
            pool.dma_start(gbc[:, 0, :], g_attn_pre.to_broadcast([P, D])).then_inc(gain_pre_in, 16)
            pool.dma_start(gbc[:, 1, :], g_attn_post.to_broadcast([P, D])).then_inc(gain_post_in, 16)
            pool.dma_start(nbc[:, 0:Q_LORA], q_norm_g.to_broadcast([P, Q_LORA])).then_inc(nbc_in, 16)
            pool.dma_start(nbc[:, Q_LORA:], kv_norm_g.to_broadcast([P, KV_LORA])).then_inc(nbc_in, 16)
            rpb = na_rpb[0]
            for par in range(2):
                for hd in range(NA_H):
                    src = bass.AP(rpb.tensor, rpb.offset + hd * RPB_R * RPB_C + (5 - par) * RPB_C + 16 - GRID,
                                  [[1, GRID], [RPB_C, 6], [1, GRID]])
                    pool.dma_start(tab_back[par * GRID:(par + 1) * GRID, hd], src).then_inc(rpb_in, 16)
            for tt in range(TT):
                pool.dma_start(gates[:, tt, :], b_gate.to_broadcast([P, 2 * D])).then_inc(bgate_in, 16)
            pool.dma_start(b1t[:], b1[0].rearrange("e (p q) -> p e q", p=P)).then_inc(b1_in, 16)
            pool.wait_ge(con_in, 32)
            pool.memset(ptab[:], 0.0).then_inc(pool_q, 1)
            seq = [1]

            def link(ins):
                seq[0] += 1
                ins.then_inc(pool_q, 1)
                pool.wait_ge(pool_q, seq[0])

            def rope(view, heads, tt):
                xv = view.rearrange("p h (a s f) -> p h a s f", a=2, s=2)
                x1v, x2v = xv[:, :, :, 0, :], xv[:, :, :, 1, :]
                n = heads * 16
                tb = [con[:, o + 16 * tt:o + 16 * tt + 16].rearrange("p (a f) -> p a f", a=2).unsqueeze(1)
                      .to_broadcast([P, heads, 2, 8]) for o in (C_COS, C_SIN)]
                t4 = [rope_s[:, i, 0:n].rearrange("p (h a f) -> p h a f", a=2, f=8) for i in range(4)]
                pool.tensor_tensor(t4[0], x1v, tb[0], ALU.mult)
                pool.tensor_tensor(t4[1], x2v, tb[1], ALU.mult)
                pool.tensor_tensor(t4[2], x1v, tb[1], ALU.mult)
                link(pool.tensor_tensor(t4[3], x2v, tb[0], ALU.mult))
                pool.tensor_tensor(x1v, t4[0], t4[1], ALU.subtract)
                return pool.tensor_tensor(x2v, t4[2], t4[3], ALU.add)

            for tt in range(TT):
                drained(pool, "lat", tt, 1)
                link(rope(lat[:, tt, Q_LORA + KV_LORA:LAT].unsqueeze(1), 1, tt))
                if tt == 0:
                    drained(pool, "tab", NA_H * 6 * GRID // BANK - 1)
                pool.tensor_copy(k96[:, tt, :, NOPE:QK], lat[:, tt, Q_LORA + KV_LORA:LAT].unsqueeze(1)
                                 .to_broadcast([P, M_H, ROPE])).then_inc(krope, 1)
            for tt in range(TT):
                drained(pool, "uq", tt, 1)
                rope(qm[:, tt, :].rearrange("p (h d) -> p h d", d=QK)[:, :, NOPE:QK], M_H, tt).then_inc(qrope, 1)
                pool.wait_ge(qrope, tt + 1)
            for i in range(2, 6):
                start_acc(i)
                if i == 2:
                    filled(pool, "hT", 0, 0)
                    pool.dma_start(gbc[:, 0, :], g_ffn_pre.to_broadcast([P, D])).then_inc(gain_pre_in, 16)
                if i == 4:
                    drained(pool, "mod", 2, 1)
                    pool.dma_start(gbc[:, 1, :], g_ffn_post.to_broadcast([P, D])).then_inc(gain_post_in, 16)
            pool.wait_ge(exps, 16)
            pool.wait_ge(pv, 16)
            pool.wait_ge(negmax, 16)
            pool.dma_start(wr[:], w_router[0].rearrange("(k p) e -> p k e", p=P)).then_inc(router_in, 16)
            pool.dma_start(brc[:], b_router.to_broadcast([P, NE])).then_inc(router_in, 16)
            pool.dma_start(b2sb[:], b2[0]).then_inc(b2_in, 16)
            pool.wait_ge(x1_made, 2)
            pool.dma_start(saved_x, xt[:]).then_inc(x_saved, 16)
            drained(pool, "mod", 5, 1)
            pool.dma_start(saved_g, modv[:, 1, :]).then_inc(g_saved, 16)
            pool.wait_ge(b1_in, 16)

            def lo_part(e, b, j, r):
                pool.wait_ge(hi_ready, unit_no(e, j) + r * UNITS + 1)
                q, s = split_slot(e, j), ring_slot(e, b, j, NF)
                pool.tensor_tensor(ring_lo[:, s], ring[:, s], whi[:, q].bitcast(F32), ALU.subtract).then_inc(lo_pool, 1)

            def sweep(r):
                def own(ins, value):
                    ins.then_inc(pool_m, 1)
                    pool.wait_ge(pool_m, value)
                    apart()

                def apart():
                    pool.nop(nofuse=True)

                def selection(e, first):
                    n0 = first
                    own(pool.tensor_copy(scS[:], ptab[:, e, :] if isinstance(e, int) else ptab[:, bass.ds(e, 1), :].squeeze(1)), n0 + 1)
                    for tt in range(TT):
                        pos, a, na = (scS[:, 5 * tt + q:5 * tt + q + 1] for q in range(3))
                        pool.tensor_scalar(sel_t[:, tt], iota, pos, na, ALU.is_equal, ALU.mult)
                        own(pool.tensor_scalar(sela_t[:, tt], iota_mod, pos, a, ALU.is_equal, ALU.mult), n0 + 2 + tt)
                        ins = pool.tensor_tensor(sel_t[:, tt, 0:HALF], sel_t[:, tt, 0:HALF].bitcast(F32),
                                                 sela_t[:, tt, 0:HALF].bitcast(F32), ALU.add)
                    ins.then_inc(sel_made, 1)
                    pool.wait_ge(sel_made, r * (NE + 1) + e + 1)

                def parameters(e, first):
                    row = (lambda t: t[:, e, :]) if isinstance(e, int) else (lambda t: t[:, bass.ds(e, 1), :].squeeze(1))
                    pool.tensor_copy(b1c[:], row(b1t))
                    pool.tensor_copy(scW[:], row(ptab)).then_inc(par_made, 1)
                    pool.wait_ge(par_made, r * NE + e + 1)
                    apart()
                    own(pool.tensor_scalar(tmpP[:], offdiag, scW[:, 1:2], None, ALU.mult), first + 1)
                    pool.tensor_tensor(fmat[:], tmpP[:], ident, ALU.add).then_inc(fold_made, 1)
                    pool.wait_ge(fold_made, r * NE + e + 1)
                    apart()

                def shares(e, first):
                    for tt in range(TT):
                        pos, ga, gb = (scW[:, 5 * tt + q:5 * tt + q + 1] for q in (0, 3, 4))
                        pool.tensor_scalar(tmpP[:], iota_mod, pos, ga, ALU.is_equal, ALU.mult)
                        own(pool.tensor_scalar(wsel[:, tt], iota, pos, gb, ALU.is_equal, ALU.mult), first + 1 + 2 * tt)
                        ins = pool.tensor_tensor(wsel[:, tt], wsel[:, tt], tmpP[:], ALU.add)
                        if tt == 0:
                            own(ins, first + 2)
                    ins.then_inc(w_made, 1)
                    pool.wait_ge(w_made, r * NE + e + 1)

                SEL, SHARES, PAR = 3, 3, 1
                b0 = r * ((SEL + SHARES + PAR) * NE + SEL)

                def first_lo(m):
                    pool.wait_ge(hi_ready, r * UNITS + m + 1)
                    s = (NF + m) % SLOTS
                    pool.tensor_tensor(ring_lo[:, s], ring[:, s], whi[:, m % SPLITS].bitcast(F32), ALU.subtract).then_inc(lo_pool, 1)

                if r == 0:
                    pool.wait_ge(tabs_made, 1)
                else:
                    pool.wait_ge(tabs_made, 2)
                    pool.wait_ge(misc_full, FILLS)
                    pool.wait_ge(u_ready, NE)
                selection(0, b0)
                first_lo(0)
                first_lo(3)
                pool.wait_ge(gather_full, r * 4 * NE + 4)
                selection(1, b0 + SEL)
                parameters(0, b0 + 2 * SEL)
                first_lo(6)
                pool.wait_ge(gather_full, r * 4 * NE + 8)
                selection(2, b0 + 2 * SEL + PAR)
                lo_part(0, 0, 1, r)

                def step(e, b):
                    base = b0 + (SEL + SHARES + PAR) * e + 3 * SEL + PAR - (SEL if last(e) else 0)
                    mine = lo_units(e, True)[1:]
                    if not no_gather(e):
                        pool.wait_ge(gather_full, r * 4 * NE + 4 * (e + 3))
                        selection(e + 3, base)
                        base = base + SEL
                    for j in mine[0:1]:
                        lo_part(e, b, j, r)
                    if not first_step(e):
                        pool.wait_ge(misc_full, r * FILLS + fill_no(e, "w") + 1)
                        apart()
                    shares(e, base)
                    for j in mine[1:]:
                        lo_part(e, b, j, r)
                    if not last(e):
                        pool.wait_ge(u_ready, r * NE + e + 1)
                        parameters(e + 1, base + SHARES)
                        lo_part(e + 1, 1 - b, lo_units(e + 1, True)[0], r)

                over_experts(pool, step)

            two_sweeps(pool, sweep)

        @block.scalar
        def _(act):
            act.wait_ge(c_in, 16)
            act.activation(st[:, 8:16], st[:, 0:8], ACT.Sigmoid).then_inc(csig, 1)

            def squares(parts, g):
                for i, (src, junk, width) in enumerate(parts):
                    ins = act.activation(junk, src, ACT.Square, scale=float(width) ** -0.5,
                                         accum_out=st[:, 32 + 4 * g + i:33 + 4 * g + i])
                ins.then_inc(ms, 1)

            def roots(g, n):
                act.wait_ge(var, g + 1)
                act.activation(st[:, 56 + 4 * g:56 + 4 * g + n], st[:, 56 + 4 * g:56 + 4 * g + n], ACT.Sqrt).then_inc(rstd, 1)

            act.wait_ge(x_in, 16)
            squares([(xt[:, tt], h[:, tt], D) for tt in range(TT)], 0)
            roots(0, 2)
            for half in range(2):
                b = take(act, "act", "mod", 0, half)
                act.activation(modv[:, 0, half * BANK:(half + 1) * BANK], b[:], ACT.Copy).then_inc(out_act, 1)
            for tt in range(TT):
                b = take(act, "act", "hT", tt, 0)
                act.activation(hT[:, 0:4, tt * P:(tt + 1) * P], b[:].rearrange("p (c t) -> p c t", c=4), ACT.Copy).then_inc(out_act, 1)
            for tt in range(TT):
                b = take(act, "act", "lat", tt, 1)
                act.activation(lat[:, tt, BANK:LAT], b[:, 0:LAT - BANK], ACT.Copy).then_inc(out_act, 1)
            drained(act, "lat", 0, 0)
            drained(act, "lat", 1, 0)
            drained(act, "lat", 1, 1)
            drained(act, "hT", 1, 1)
            filled(act, "hT", 1, 1)
            squares([(lat[:, tt, 0:Q_LORA], h[:, 0, tt * Q_LORA:(tt + 1) * Q_LORA], Q_LORA) for tt in range(TT)]
                    + [(lat[:, tt, Q_LORA:Q_LORA + KV_LORA], h[:, tt, (1 - tt) * 2 * Q_LORA:][:, 0:KV_LORA], KV_LORA) for tt in range(TT)], 1)
            roots(1, 4)
            for name, dst in (("q", qT), ("k", kT)):
                for cc in range(4):
                    b = take(act, "act", name, cc)
                    act.activation(dst[:, cc, :], b[:, 0:TT * P], ACT.Copy).then_inc(out_act, 1)
            for tt in range(TT):
                b = take(act, "act", "ckT", tt)
                act.activation(cT[:, 3:5, tt * P:(tt + 1) * P], b[:, 0:2 * P].rearrange("p (c t) -> p c t", c=2), ACT.Copy).then_inc(out_act, 1)
            for tt in range(TT):
                for half in range(2):
                    b = take(act, "act", "ukv", tt, half)
                    kv = b[:].rearrange("p (h d) -> p h d", d=P)
                    act.activation(k96[:, tt, 4 * half:4 * half + 4, 0:NOPE], kv[:, :, 0:NOPE], ACT.Copy)
                    act.activation(v_m[:, tt, half * 256:(half + 1) * 256].rearrange("p (h d) -> p h d", d=64),
                                   kv[:, :, NOPE:P], ACT.Copy).then_inc(out_act, 1)
            for tt in range(TT):
                for g in range(2):
                    b = take(act, "act", "mqT", tt, g)
                    act.activation(mqT[:, 4 * g:4 * g + 4, tt * P:(tt + 1) * P], b[0:QK, :].rearrange("p (c t) -> p c t", c=4), ACT.Copy).then_inc(out_act, 1)

            def softmax(n):
                act.wait_ge(negmax, n + 1)
                if n >= 2:
                    filled(act, "pT", n - 2)
                for hh in range(2):
                    ins = act.activation(p_sb[:, n % 2, hh], s_sb[:, n % 2, hh], ACT.Exp,
                                         bias=nmx[:, n % 2, hh:hh + 1], accum_out=lsum[:, 2 * n + hh:2 * n + hh + 1])
                ins.then_inc(exps, 1)

            softmax(0)
            softmax(1)
            for n in range(16):
                if n >= 2:
                    act.wait_ge(pv, n - 1)
                b = take(act, "act", "pT", n)
                act.activation(pT[:, n % 2], b[:].rearrange("p (c t) -> p c t", c=4), ACT.Copy).then_inc(out_act, 1)
                if n + 2 < 16:
                    softmax(n + 2)
                if MOD_AFTER.get(n) == 3:
                    for half in range(2):
                        b = take(act, "act", "mod", 3, half)
                        act.activation(modv[:, 0, half * BANK:(half + 1) * BANK], b[:], ACT.Copy).then_inc(out_act, 1)
            drained(act, "gate", 3, 1)
            act.activation(gates[:], gates[:], ACT.Sigmoid).then_inc(sig_made, 1)
            for a in (0, 2):
                b = take(act, "act", "oT", a)
                act.activation(oT[:, 4 * (a // 2):4 * (a // 2) + 4, (a % 2) * P:(a % 2 + 1) * P],
                               b[:].rearrange("p (c t) -> p c t", c=4), ACT.Copy).then_inc(out_act, 1)
            for tt in range(TT):
                b = take(act, "act", "mT", tt, 0)
                act.activation(hT[:, 0:4, tt * P:(tt + 1) * P], b[:].rearrange("p (c t) -> p c t", c=4), ACT.Copy).then_inc(out_act, 1)
            for tt in range(TT):
                for half in range(2):
                    b = take(act, "act", "y", tt, half)
                    act.activation(ysb[:, tt, half * BANK:(half + 1) * BANK], b[:], ACT.Copy).then_inc(out_act, 1)
            drained(act, "y", 1, 1)
            squares([(ysb[:, tt], h[:, tt], D) for tt in range(TT)], 2)
            roots(2, 2)
            act.wait_ge(x1_made, 2)
            squares([(xt[:, tt], h[:, tt], D) for tt in range(TT)], 3)
            roots(3, 2)
            for tt in range(TT):
                b = take(act, "act", "h2T", tt, 0)
                act.activation(hT[:, 0:4, tt * P:(tt + 1) * P], b[:].rearrange("p (c t) -> p c t", c=4), ACT.Copy).then_inc(out_act, 1)
            act.wait_ge(h2_made, 2)
            for tt in range(TT):
                act.activation(xs_hi[:, tt], h[:, tt, :].rearrange("p (q k) -> p k q", k=KD), ACT.Copy).then_inc(xhi_made, 1)
            act.wait_ge(nv1, 2)
            for tt in range(TT):
                ins = act.activation(rt[:, 2 + tt], rt[:, tt], ACT.Exp, bias=st[:, 80 + tt:81 + tt])
            ins.then_inc(ex_made, 1)
            for tt in range(TT):
                for half in range(2):
                    b = take(act, "act", "b2", tt, half)
                    act.activation(out_acc[:, tt, half * BANK:(half + 1) * BANK], b[:], ACT.Copy).then_inc(out_act, 1)
            act.wait_ge(x_saved, 16)
            act.wait_ge(g_saved, 16)
            act.wait_ge(xlo_made, 2)

            def hi_part(e, b, j, r, pair=None):
                m = unit_no(e, j)
                if isinstance(m, int):
                    n = NF + m + r * UNITS
                    act.wait_ge(landed[n % SLOTS], 16 * (n // SLOTS + 1))
                    slot = n % SLOTS
                else:
                    slot = ring_slot(e, b, j, NF)
                    n0 = NF + 8 + 12 * b + j + r * UNITS
                    act.wait_ge(landed[slot], 48 * pair + 16 * (n0 // SLOTS + 1))
                q = split_slot(e, j)
                if not (isinstance(m, int) and r == 0 and m < SPLITS):
                    act.wait_ge(split_used, m + r * UNITS + 1 - SPLITS)
                act.activation(whi[:, q], ring[:, slot], ACT.Copy).then_inc(hi_ready, 1)

            pair_of = {"i": None}

            def sweep(r):
                def drain_gather(g0, which_bank, q, par):
                    act.wait_ge(gather_full, r * 4 * NE + g0 + q + 1)
                    t, half = (t1, t2)[q // 2], q % 2
                    act.activation(t[:, par, 4 * half:4 * half + 4], ps[which_bank][:].rearrange("p (c t) -> p c t", c=4), ACT.Copy).then_inc(gather_used, 1)

                def first_hi(m):
                    n = NF + m + r * UNITS
                    act.wait_ge(landed[n % SLOTS], 16 * (n // SLOTS + 1))
                    if m + r * UNITS >= SPLITS:
                        act.wait_ge(split_used, m + r * UNITS + 1 - SPLITS)
                    act.activation(whi[:, m % SPLITS], ring[:, n % SLOTS], ACT.Copy).then_inc(hi_ready, 1)

                def hidden_rows(e):
                    act.wait_ge(split_used, r * UNITS + (8 if first_step(e) else unit_no(e - 1, 7) + 1))
                    for q in range(2):
                        ins = act.activation(hs[:, q * BANK:(q + 1) * BANK], ps[q][:], ACT.Copy)
                    ins.then_inc(hs_act, 1)

                def result(e, b):
                    act.wait_ge(split_used, r * UNITS + unit_no(e - 1, 11) + 1)
                    for q in range(2):
                        ins = act.activation(ys[:, q * BANK:(q + 1) * BANK], ps[4 + q][:], ACT.Copy)
                    ins.then_inc(ys_made, 1)
                    act.wait_ge(misc_full, r * FILLS + fill_no(e, "w") + 1)
                    act.activation(wT[:], ps[6 + bank_of(e, "w", b)][:, 0:TT * P], ACT.Copy).then_inc(drain_act, 1)

                for m in range(4):
                    first_hi(m)
                for q in range(4):
                    drain_gather(0, q, q, 0)
                for m in range(4, 7):
                    first_hi(m)
                for q in range(4):
                    drain_gather(4, 4 + q, q, 1)
                first_hi(7)
                hi_part(0, 0, 0, r)
                hidden_rows(0)
                for j in range(1, AHEAD):
                    hi_part(0, 0, j, r)

                def step(e, b):
                    pair = pair_of["i"]
                    mine = step_units(e)[AHEAD:]
                    if not first_step(e):
                        result(e, b)
                    if not no_gather(e):
                        for q in range(4):
                            drain_gather(4 * (e + 2), q, q, (e if isinstance(e, int) else b) % 2)
                    for j in mine[0:3]:
                        hi_part(e, b, j, r, pair)
                    act.wait_ge(glu_made, r * NE + e + 1)
                    act.activation(sg[:], hb[:, :, 0, :], ACT.Sigmoid, scale=ALPHA).then_inc(sg_made, 1)
                    for j in mine[3:5]:
                        hi_part(e, b, j, r, pair)
                    act.wait_ge(a_made, r * NE + e + 1)
                    act.activation(u1[:].rearrange("p k t -> p (k t)"), sg[:].rearrange("p f t -> p (f t)"), ACT.Copy).then_inc(u1_made, 1)
                    for j in mine[5:]:
                        hi_part(e, b, j, r, pair)
                    if not last(e):
                        following = step_units(e + 1)[:AHEAD]
                        next_pair = None if pair is None else pair + b
                        hi_part(e + 1, 1 - b, following[0], r, next_pair)
                        hidden_rows(e + 1)
                        for j in following[1:]:
                            hi_part(e + 1, 1 - b, j, r, next_pair)

                over_experts_i(act, step, pair_of)
                result(NE, 0)

            two_sweeps(act, sweep, after=lambda: act.wait_ge(drain_dve, 2 * DVE_DRAINS))
            act.wait_ge(drain_dve, DVE_DRAINS)
            act.wait_ge(a_made, NE)
            squares([(out_acc[:, tt], hs[:, 0:D] if tt == 0 else hs[:, D:2 * D], D) for tt in range(TT)], 4)
            roots(4, 2)

        @block.vector
        def _(dve):
            seq = [0]

            def link(ins):
                seq[0] += 1
                ins.then_inc(dve_q, 1)
                dve.wait_ge(dve_q, seq[0])

            dve.wait_ge(csig, 1)
            link(dve.tensor_tensor(st[:, 16:24], st[:, 0:8], st[:, 8:16], ALU.mult))

            def ada_unit(i, u):
                v = (0, 1, *ADA_LATE)[i]
                arrived(dve, "ada", v, u)
                if u == 0:
                    dve.wait_ge(ada_row[i % 2], 16 * (i // 2 + 1))
                src = unit_at("ada", v, u).rearrange("p (k n) -> p k n", k=2)
                for q in range(2):
                    k = 2 * u + q
                    ins = dve.scalar_tensor_tensor(acc[:, i % 2], src[:, q], st[:, 16 + k:17 + k], acc[:, i % 2], ALU.mult, ALU.add)
                    if q == 0:
                        link(ins)
                ins.then_inc(ada_used, 1)
                dve.wait_ge(ada_used, 4 * i + u + 1)

            def inverse(g, n):
                dve.wait_ge(ms, g + 1)
                link(dve.tensor_scalar(st[:, 32 + 4 * g:32 + 4 * g + n], st[:, 32 + 4 * g:32 + 4 * g + n], EPS, None, ALU.add))
                dve.reciprocal(st[:, 56 + 4 * g:56 + 4 * g + n], st[:, 32 + 4 * g:32 + 4 * g + n]).then_inc(var, 1)

            def root(g, i):
                return st[:, 56 + 4 * g + i:57 + 4 * g + i]

            def mod_drain(v):
                for half in range(2):
                    b = take(dve, "dve", "mod", v, half)
                    dst, gain = modv[:, MODV[v], half * BANK:(half + 1) * BANK], gbc[:, 1 if v in (2, 5) else 0, half * BANK:(half + 1) * BANK]
                    if v in (1, 4):
                        dve.scalar_tensor_tensor(dst, b[:], 1.0, gain, ALU.add, ALU.mult).then_inc(out_dve, 1)
                    else:
                        dve.tensor_tensor(dst, b[:], gain, ALU.mult).then_inc(out_dve, 1)

            inverse(0, 2)
            for u in range(4):
                ada_unit(0, u)
            for u in range(4):
                ada_unit(1, u)
            dve.wait_ge(gain_pre_in, 16)
            mod_drain(1)
            dve.wait_ge(rstd, 1)
            drained(dve, "mod", 1, 1)
            drained(dve, "mod", 0, 1)

            def norm_in(src, g, shift_sem):
                for tt in range(TT):
                    link(dve.scalar_tensor_tensor(h[:, tt], src[:, tt], root(g, tt), modv[:, MODV[4] if g else MODV[1]], ALU.mult, ALU.mult))
                    dve.tensor_tensor(h[:, tt], h[:, tt], modv[:, 0], ALU.add).then_inc(shift_sem, 1)

            norm_in(xt, 0, h_made)
            for tt in range(TT):
                b = take(dve, "dve", "hT", tt, 1)
                dve.tensor_copy(hT[:, 4:8, tt * P:(tt + 1) * P], b[:].rearrange("p (c t) -> p c t", c=4)).then_inc(out_dve, 1)
            for tt in range(TT):
                b = take(dve, "dve", "lat", tt, 0)
                dve.tensor_copy(lat[:, tt, 0:BANK], b[:]).then_inc(out_dve, 1)
            inverse(1, 4)
            dve.wait_ge(con_in, 32)
            mask = con[:, C_MASK:C_MASK + GRID].unsqueeze(1).to_broadcast([P, BANK // GRID, GRID])
            tab_rows = tab[:].rearrange("p h r c -> p (h r) c")
            for i in range(NA_H * 6 * GRID // BANK):
                b = take(dve, "dve", "tab", i)
                dve.tensor_tensor(tab_rows[:, i * (BANK // GRID):(i + 1) * (BANK // GRID)], b[:].rearrange("p (r c) -> p r c", c=GRID), mask, ALU.add).then_inc(out_dve, 1)
            dve.wait_ge(rstd, 2)
            dve.wait_ge(nbc_in, 32)
            for tt in range(TT):
                a, z = lat[:, tt, 0:Q_LORA], lat[:, tt, Q_LORA:Q_LORA + KV_LORA]
                dve.scalar_tensor_tensor(a, a, root(1, tt), nbc[:, 0:Q_LORA], ALU.mult, ALU.mult)
                dve.scalar_tensor_tensor(z, z, root(1, 2 + tt), nbc[:, Q_LORA:], ALU.mult, ALU.mult).then_inc(lat_made, 1)
            for tt in range(TT):
                b = take(dve, "dve", "v", tt)
                dve.tensor_copy(v_na[:, tt], b[:]).then_inc(out_dve, 1)
            for tt in range(TT):
                b = take(dve, "dve", "cqT", tt)
                dve.tensor_copy(cT[:, 0:3, tt * P:(tt + 1) * P], b[:, 0:3 * P].rearrange("p (c t) -> p c t", c=3)).then_inc(out_dve, 1)
            for tt in range(TT):
                for half in range(2):
                    b = take(dve, "dve", "uq", tt, half)
                    dve.tensor_copy(qm[:, tt, half * 384:(half + 1) * 384], b[:, 0:384]).then_inc(out_dve, 1)
            for tt in range(TT):
                for g in range(2):
                    b = take(dve, "dve", "mkT", tt, g)
                    dve.tensor_copy(mkT[:, 4 * g:4 * g + 4, tt * P:(tt + 1) * P], b[0:QK, :].rearrange("p (c t) -> p c t", c=4)).then_inc(out_dve, 1)

            def scores(n):
                br, tt, hp = n // 8, n // 4 % 2, n % 4
                b = take(dve, "dve", "s", n)
                if n >= 2:
                    dve.wait_ge(exps, n - 1)
                if n == 0:
                    drained(dve, "tab", NA_H * 6 * GRID // BANK - 1)
                    filled(dve, "mqT", 1, 1)
                if br == 0:
                    j0 = 2 - 2 * tt
                    ins = dve.scalar_tensor_tensor(s_sb[:, n % 2], b[:].rearrange("p (h k) -> p h k", h=2), NA_D ** -0.5,
                                                   tab[:, 2 * hp:2 * hp + 2, j0:j0 + 4, :].rearrange("p h r c -> p h (r c)"), ALU.mult, ALU.add)
                else:
                    ins = dve.tensor_scalar(s_sb[:, n % 2], b[:].rearrange("p (h k) -> p h k", h=2), QK ** -0.5, None, ALU.mult)
                ins.then_inc(out_dve, 1)
                drained(dve, "s", n)
                link(dve.tensor_reduce(mx[:, n % 2], s_sb[:, n % 2], AX, ALU.max))
                dve.tensor_scalar(nmx[:, n % 2], mx[:, n % 2], -1.0, None, ALU.mult).then_inc(negmax, 1)

            scores(0)
            scores(1)
            for n in range(16):
                ada_unit(2 + n // 4, n % 4)
                if n + 2 < 16:
                    scores(n + 2)
                if n % 4 == 3:
                    a = n // 4
                    dve.wait_ge(exps, n + 1)
                    link(dve.reciprocal(linv[:, 8 * a:8 * a + 8], lsum[:, 8 * a:8 * a + 8]))
                    b = take(dve, "dve", "o", a)
                    dve.tensor_tensor(o_sb[:, a].rearrange("p (h d) -> p h d", d=64), b[:].rearrange("p (h d) -> p h d", d=64),
                                      linv[:, 8 * a:8 * a + 8].unsqueeze(2).to_broadcast([P, 8, 64]), ALU.mult).then_inc(out_dve, 1)
                if n % 4 == 2:
                    if n == 2:
                        dve.wait_ge(bgate_in, 16 * TT)
                    for tt in range(TT):
                        b = take(dve, "dve", "gate", n // 4, tt)
                        g = gates[:, tt, (n // 4) * BANK:(n // 4 + 1) * BANK]
                        dve.tensor_tensor(g, b[:], g, ALU.add).then_inc(out_dve, 1)
                if n in MOD_AFTER and MOD_AFTER[n] != 3:
                    if MOD_AFTER[n] == 4:
                        dve.wait_ge(gain_pre_in, 32)
                    else:
                        dve.wait_ge(gain_post_in, 16 if MOD_AFTER[n] == 2 else 32)
                    mod_drain(MOD_AFTER[n])
            for a in (1, 3):
                b = take(dve, "dve", "oT", a)
                dve.tensor_copy(oT[:, 4 * (a // 2):4 * (a // 2) + 4, (a % 2) * P:(a % 2 + 1) * P],
                                b[:].rearrange("p (c t) -> p c t", c=4)).then_inc(out_dve, 1)
            dve.wait_ge(sig_made, 1)
            for br in range(2):
                for tt in range(TT):
                    for half in range(2):
                        b = take(dve, "dve", "up", br, tt, half)
                        g = gates[:, tt, br * D + half * BANK:br * D + (half + 1) * BANK]
                        m = h[:, tt, half * BANK:(half + 1) * BANK]
                        if br == 0:
                            dve.tensor_tensor(m, b[:], g, ALU.mult).then_inc(out_dve, 1)
                        else:
                            dve.tensor_tensor(g, b[:], g, ALU.mult).then_inc(out_dve, 1)
                            drained(dve, "up", br, tt, half)
                            dve.tensor_tensor(m, m, g, ALU.add).then_inc(merged_s, 1)
            for tt in range(TT):
                b = take(dve, "dve", "mT", tt, 1)
                dve.tensor_copy(hT[:, 4:8, tt * P:(tt + 1) * P], b[:].rearrange("p (c t) -> p c t", c=4)).then_inc(out_dve, 1)
            inverse(2, 2)
            dve.wait_ge(rstd, 3)
            for tt in range(TT):
                link(dve.scalar_tensor_tensor(ysb[:, tt], ysb[:, tt], root(2, tt), modv[:, MODV[2]], ALU.mult, ALU.mult))
                dve.tensor_tensor(xt[:, tt], xt[:, tt], ysb[:, tt], ALU.add).then_inc(x1_made, 1)
            inverse(3, 2)
            dve.wait_ge(rstd, 4)
            drained(dve, "mod", 3, 1)
            norm_in(xt, 3, h2_made)
            for tt in range(TT):
                b = take(dve, "dve", "h2T", tt, 1)
                dve.tensor_copy(hT[:, 4:8, tt * P:(tt + 1) * P], b[:].rearrange("p (c t) -> p c t", c=4)).then_inc(out_dve, 1)
            L, EX, GT, EQ, CUM, MASK, GATE, TMP = 0, 2, 4, 6, 8, 10, 12, 14
            dve.wait_ge(router_in, 32)
            for tt in range(TT):
                b = take(dve, "dve", "lg", tt)
                ins = dve.tensor_tensor(rt[:, L + tt], b[:, 0:NE], brc[:], ALU.add)
                ins.then_inc(out_dve, 1)
                drained(dve, "lg", tt)
                link(dve.max(m8[:, tt], rt[:, L + tt]))
                dve.tensor_scalar(st[:, 80 + tt:81 + tt], m8[:, tt, 0:1], -1.0, None, ALU.mult).then_inc(nv1, 1)
                v4 = m8[:, tt, TOPK - 1:TOPK]
                dve.tensor_scalar(rt[:, GT + tt], rt[:, L + tt], v4, None, ALU.is_gt)
                link(dve.tensor_scalar(rt[:, EQ + tt], rt[:, L + tt], v4, None, ALU.is_equal))
                dve.tensor_reduce(st[:, 82 + tt:83 + tt], rt[:, GT + tt], AX, ALU.add)
                link(dve.tensor_tensor_scan(rt[:, CUM + tt], ones[:, 0:NE], rt[:, EQ + tt], 0.0, ALU.mult, ALU.add))
                link(dve.tensor_scalar(st[:, 84 + tt:85 + tt], st[:, 82 + tt:83 + tt], -1.0, float(TOPK), ALU.mult, ALU.add))
                link(dve.scalar_tensor_tensor(rt[:, CUM + tt], rt[:, CUM + tt], st[:, 84 + tt:85 + tt], rt[:, EQ + tt], ALU.is_le, ALU.mult))
                dve.tensor_tensor(rt[:, MASK + tt], rt[:, GT + tt], rt[:, CUM + tt], ALU.add).then_inc(mask_made, 1)
            dve.wait_ge(mask_made, 2)
            dve.wait_ge(ex_made, 1)
            for tt in range(TT):
                link(dve.tensor_tensor(rt[:, TMP + tt], rt[:, EX + tt], rt[:, MASK + tt], ALU.mult))
                link(dve.tensor_reduce(st[:, 86 + tt:87 + tt], rt[:, TMP + tt], AX, ALU.add))
                link(dve.reciprocal(st[:, 86 + tt:87 + tt], st[:, 86 + tt:87 + tt]))
                dve.tensor_scalar(rt[:, GATE + tt], rt[:, TMP + tt], st[:, 86 + tt:87 + tt], None, ALU.mult).then_inc(gate_made, 1)
            dve.wait_ge(pool_q, 1)
            pt = ptab[:, 0:NE, :]
            for tt in range(TT):
                b = take(dve, "dve", "pos", tt)
                dve.scalar_tensor_tensor(rt[:, EQ + tt], b[:, 0:NE], 1.0, rt[:, MASK + tt], ALU.add, ALU.mult).then_inc(out_dve, 1)
                drained(dve, "pos", tt)
                dve.tensor_scalar(pt[:, :, 5 * tt], rt[:, EQ + tt], -1.0, None, ALU.add)
            b = take(dve, "dve", "cnt")
            dve.tensor_copy(rt[:, TMP], b[:, 0:NE]).then_inc(out_dve, 1)
            drained(dve, "cnt")
            dve.wait_ge(gate_made, 2)
            dve.tensor_copy(cnt_i[:], rt[:, TMP])
            for tt in range(TT):
                dve.tensor_scalar(pt[:, :, 5 * tt + 1], rt[:, TMP], float(half_cap), None, ALU.is_le)
                dve.tensor_scalar(pt[:, :, 5 * tt + 2], rt[:, TMP], float(half_cap), None, ALU.is_gt)
                dve.scalar_tensor_tensor(pt[:, :, 5 * tt + 3], rt[:, TMP], float(half_cap), rt[:, GATE + tt], ALU.is_le, ALU.mult)
                dve.scalar_tensor_tensor(pt[:, :, 5 * tt + 4], rt[:, TMP], float(half_cap), rt[:, GATE + tt], ALU.is_gt, ALU.mult)
            link(dve.tensor_reduce(st[:, 88:89], rt[:, TMP], AX, ALU.max))
            dve.tensor_copy(ovf_i[:], st[:, 88:89]).then_inc(tabs_made, 1)
            for tt in range(TT):
                b = take(dve, "dve", "gT", tt)
                dve.tensor_copy(gT[:, tt * P:(tt + 1) * P], b[0:NE, 0:P]).then_inc(out_dve, 1)
            for tt in range(TT):
                dve.wait_ge(xhi_made, tt + 1)
                dve.tensor_tensor(xs_lo[:, tt], h[:, tt, :].rearrange("p (q k) -> p k q", k=KD), xs_hi[:, tt].bitcast(F32), ALU.subtract).then_inc(xlo_made, 1)
            drained(dve, "b2", 1, 1)

            def lo_part(e, b, j, r):
                dve.wait_ge(hi_ready, unit_no(e, j) + r * UNITS + 1)
                q, s = split_slot(e, j), ring_slot(e, b, j, NF)
                dve.tensor_tensor(ring_lo[:, s], ring[:, s], whi[:, q].bitcast(F32), ALU.subtract).then_inc(lo_dve, 1)

            def sweep(r):
                fb, db, eb = r * FILLS, r * DVE_DRAINS, r * NE

                def hidden_rows(e):
                    dve.wait_ge(split_used, r * UNITS + (8 if first_step(e) else unit_no(e - 1, 7) + 1))
                    for q in (2, 3):
                        ins = dve.tensor_copy(hs[:, q * BANK:(q + 1) * BANK], ps[q][:])
                    ins.then_inc(hs_dve, 1)

                def combine(e, b):
                    if not (isinstance(e, int) and e == 1 and r == 0):
                        dve.wait_ge(drain_dve, db + (8 * e - 4 if isinstance(e, int) and e == NE else 8 * e))
                    for q in range(4):
                        dve.wait_ge(misc_full, fb + fill_no(e, "c%d" % q) + 1)
                        dst = out_acc[:, q // 2, (q % 2) * BANK:(q % 2 + 1) * BANK]
                        dve.tensor_tensor(dst, ps[6 + bank_of(e, "c%d" % q, b)][:], dst, ALU.add).then_inc(drain_dve, 1)

                for m in (1, 2, 4, 5, 7):
                    dve.wait_ge(hi_ready, r * UNITS + m + 1)
                    s = (NF + m) % SLOTS
                    dve.tensor_tensor(ring_lo[:, s], ring[:, s], whi[:, m % SPLITS].bitcast(F32), ALU.subtract).then_inc(lo_dve, 1)
                hidden_rows(0)
                lo_part(0, 0, 0, r)

                def step(e, b):
                    mine = lo_units(e, False)[1:]
                    for j in mine[0:1]:
                        lo_part(e, b, j, r)
                    dve.wait_ge(par_made, eb + e + 1)
                    if not (first_step(e) and r == 0):
                        dve.wait_ge(u_ready, eb + e)
                        dve.wait_ge(u1_made, eb + e)
                    for f in range(4):
                        dve.wait_ge(misc_full, fb + fill_no(e, "f%d" % f) + 1)
                        bias = b1c[:].rearrange("p (k g) -> p g k", g=2)[:, :, 2 * f:2 * f + 2].unsqueeze(3).to_broadcast([P, 2, 2, P])
                        dve.tensor_tensor(hb[:, f].rearrange("p g (k t) -> p g k t", k=2),
                                          ps[6 + bank_of(e, "f%d" % f, b)][:].rearrange("p (g k t) -> p g k t", g=2, k=2), bias, ALU.add).then_inc(drain_dve, 1)
                    dve.wait_ge(drain_dve, db + drains(e, "f3")[1])
                    glu, lin = hb[:, :, 0, :], hb[:, :, 1, :]
                    dve.tensor_scalar(glu, glu, LIMIT, None, ALU.min).then_inc(glu_made, 1)
                    dve.tensor_scalar(lin, lin, LIMIT, -LIMIT, ALU.min, ALU.max).then_inc(lin_made, 1)
                    if not first_step(e):
                        combine(e, b)
                    for j in mine[1:2]:
                        lo_part(e, b, j, r)
                    dve.wait_ge(sg_made, eb + e + 1)
                    dve.tensor_tensor(sg[:], sg[:], glu, ALU.mult).then_inc(a1_made, 1)
                    dve.wait_ge(a1_made, eb + e + 1)
                    dve.wait_ge(lin_made, eb + e + 1)
                    dve.scalar_tensor_tensor(sg[:], lin, 1.0, sg[:], ALU.add, ALU.mult).then_inc(a_made, 1)
                    for j in mine[2:3]:
                        lo_part(e, b, j, r)
                    dve.wait_ge(u1_made, eb + e + 1)
                    u1f, u2f = u1[:].rearrange("p k t -> p (k t)"), u2[:].rearrange("p k t -> p (k t)")
                    dve.tensor_tensor(u2f, sg[:].rearrange("p f t -> p (f t)"), u1f.bitcast(F32), ALU.subtract).then_inc(u2_made, 1)
                    dve.wait_ge(u2_made, eb + e + 1)
                    dve.nop(nofuse=True)
                    a_half = sg[:].rearrange("p f (k t) -> p (f k) t", k=2)[:, :, HALF:P]
                    dve.copy_predicated(a_half, scW[:, 1:2].bitcast(U32).unsqueeze(1).to_broadcast([P, KD, HALF]),
                                        u2[:, :, HALF:P].bitcast(F32)).then_inc(picked, 1)
                    dve.wait_ge(picked, eb + e + 1)
                    dve.tensor_copy(u1[:, :, HALF:P], a_half).then_inc(u_ready, 1)
                    for j in mine[3:6]:
                        lo_part(e, b, j, r)
                    if not last(e):
                        hidden_rows(e + 1)
                    for j in mine[6:]:
                        lo_part(e, b, j, r)
                    if not last(e):
                        lo_part(e + 1, 1 - b, lo_units(e + 1, False)[0], r)

                over_experts(dve, step)
                combine(NE, 0)

            def more_positions():
                dve.wait_ge(w_made, NE)
                for tt in range(TT):
                    dve.tensor_scalar(pt[:, :, 5 * tt], pt[:, :, 5 * tt], -float(full), None, ALU.add)
                    dve.tensor_tensor(pt[:, :, 5 * tt + 4], pt[:, :, 5 * tt + 3], pt[:, :, 5 * tt + 4], ALU.add).then_inc(gates_joined, 1)
                dve.wait_ge(gates_joined, TT)
                for tt in range(TT):
                    dve.memset(pt[:, :, 5 * tt + 3], 0.0)
                    dve.memset(pt[:, :, 5 * tt + 1], 0.0)
                    dve.memset(pt[:, :, 5 * tt + 2], 1.0)
                dve.tensor_copy(st[:, 90:91], st[:, 88:89]).then_inc(tabs_made, 1)

            two_sweeps(dve, sweep, more_positions, lambda: dve.wait_ge(drain_dve, 2 * DVE_DRAINS))
            dve.wait_ge(drain_dve, DVE_DRAINS)
            inverse(4, 2)
            dve.wait_ge(rstd, 5)
            dve.wait_ge(back_in, 32)
            for tt in range(TT):
                link(dve.scalar_tensor_tensor(out_acc[:, tt], out_acc[:, tt], root(4, tt), gf[:], ALU.mult, ALU.mult))
                dve.tensor_tensor(y_out[:, tt], out_acc[:, tt], res[:, tt], ALU.add).then_inc(fin, 1)

        @block.tensor
        def _(pe):
            pe.wait_ge(con_in, 32)
            def mod(v):
                i = (0, 1, *ADA_LATE).index(v)
                pe.wait_ge(ada_used, 4 * i + 4)
                for half in range(2):
                    b = open_bank(pe, "mod", v, half)
                    pe.matmul(b[:], ones, acc[:, i % 2, half * BANK:(half + 1) * BANK], start=True, stop=True).then_inc(full_f, 1)

            def turn_tile(name, src, ready, n):
                for tt in range(TT):
                    pe.wait_ge(ready, n * (tt + 1))
                    for q in range(2):
                        b = open_bank(pe, name, tt, q)
                        for cc in range(4):
                            ins = pe.transpose(b[:, cc * P:(cc + 1) * P], src[:, tt, (4 * q + cc) * P:(4 * q + cc + 1) * P], ident)
                        ins.then_inc(full_f, 1)

            mod(0)
            mod(1)
            turn_tile("hT", h, h_made, 1)
            for tt in range(TT):
                for q in range(2):
                    drained(pe, "hT", tt, q)

            def hidden(tt, k):
                return hT[:, k, tt * P:(tt + 1) * P]

            lat_banks = [[open_bank(pe, "lat", tt, part) for part in range(2)] for tt in range(TT)]
            for u in range(3):
                arrived(pe, "lat", u)
                ks = range(3 * u, min(KD, 3 * u + 3))
                view = unit_at("lat", u)[:, 0:len(ks) * LAT].rearrange("p (k n) -> p k n", k=len(ks))
                for tt in range(TT):
                    for part, (c0, c1) in enumerate(((0, BANK), (BANK, LAT))):
                        for i, k in enumerate(ks):
                            ins = pe.matmul(lat_banks[tt][part][:, 0:c1 - c0], hidden(tt, k), view[:, i, c0:c1], start=(k == 0), stop=(k == KD - 1))
                        if u == 2:
                            ins.then_inc(full_f, 1)
                if u < 2:
                    ins.then_inc(pe_used, 1)
            pe.wait_ge(rpb_in, 16 * 2 * NA_H)
            back = tab_back[:].rearrange("p h r c -> p (h r c)")
            for i in range(NA_H * 6 * GRID // BANK):
                b = open_bank(pe, "tab", i)
                pe.matmul(b[:], flip[:], back[:, i * BANK:(i + 1) * BANK], start=True, stop=True).then_inc(full_f, 1)

            for name in "qk":
                banks = [open_bank(pe, name, cc) for cc in range(4)]
                for u in range(2):
                    arrived(pe, name, u)
                    view = unit_at(name, u).rearrange("p (k n) -> p k n", k=4)
                    for cc in range(4):
                        for i in range(4):
                            ins = pe.matmul(banks[cc][:, 0:TT * P], view[:, i, cc * P:(cc + 1) * P], hT[:, 4 * u + i, :], start=(u == 0 and i == 0), stop=(u == 1 and i == 3))
                        if u == 1:
                            ins.then_inc(full_f, 1)
                    if u == 0:
                        ins.then_inc(pe_used, 1)

            def two_tiles(name, keys, k_units):
                banks = [open_bank(pe, *key) for key in keys]
                for u in range(k_units):
                    arrived(pe, *name, u)
                    view = unit_at(*name, u).rearrange("p (k n) -> p k n", k=4)
                    for tt in range(TT):
                        for i in range(4):
                            ins = pe.matmul(banks[tt][:], hidden(tt, 4 * u + i), view[:, i], start=(u == 0 and i == 0), stop=(u == 1 and i == 3))
                        if u == k_units - 1:
                            ins.then_inc(full_f, 1)
                    if u < k_units - 1:
                        ins.then_inc(pe_used, 1)

            two_tiles(("v",), [("v", tt) for tt in range(TT)], 2)
            for tt in range(TT):
                pe.wait_ge(lat_made, tt + 1)
                for name, c0, nch in (("cqT", 0, 3), ("ckT", 3, 2)):
                    b = open_bank(pe, name, tt)
                    for cc in range(nch):
                        ins = pe.transpose(b[:, cc * P:(cc + 1) * P], lat[:, tt, (c0 + cc) * P:(c0 + cc + 1) * P], ident)
                    ins.then_inc(full_f, 1)
            for tt in range(TT):
                drained(pe, "cqT", tt)
                drained(pe, "ckT", tt)
            banks = [[open_bank(pe, "uq", tt, half) for half in range(2)] for tt in range(TT)]
            for u in range(2):
                arrived(pe, "uq", u)
                ks = ((0, 1), (2,))[u]
                view = unit_at("uq", u)[:, 0:len(ks) * M_H * QK].rearrange("p (k n) -> p k n", k=len(ks))
                for tt in range(TT):
                    for half in range(2):
                        for i, k in enumerate(ks):
                            ins = pe.matmul(banks[tt][half][:, 0:384], cT[:, k, tt * P:(tt + 1) * P], view[:, i, half * 384:(half + 1) * 384], start=(k == 0), stop=(k == 2))
                        if u == 1:
                            ins.then_inc(full_f, 1)
                if u == 0:
                    ins.then_inc(pe_used, 1)
            arrived(pe, "ukv", 0)
            view = unit_at("ukv", 0).rearrange("p (k n) -> p k n", k=2)
            for tt in range(TT):
                for half in range(2):
                    b = open_bank(pe, "ukv", tt, half)
                    for i in range(2):
                        ins = pe.matmul(b[:], cT[:, 3 + i, tt * P:(tt + 1) * P], view[:, i, half * BANK:(half + 1) * BANK], start=(i == 0), stop=(i == 1))
                    ins.then_inc(full_f, 1)
            for name, src, ready in (("mkT", k96, krope), ("mqT", qm, qrope)):
                for tt in range(TT):
                    pe.wait_ge(ready, tt + 1)
                    if name == "mkT":
                        drained(pe, "ukv", tt, 1)
                    for g in range(2):
                        b = open_bank(pe, name, tt, g)
                        for cc in range(4):
                            hd = 4 * g + cc
                            s = src[:, tt, hd, :] if name == "mkT" else src[:, tt, hd * QK:(hd + 1) * QK]
                            ins = pe.transpose(b[0:QK, cc * P:(cc + 1) * P], s, ident)
                        ins.then_inc(full_f, 1)
            for tt in range(TT):
                drained(pe, "q", 3), drained(pe, "k", 3), drained(pe, "v", tt)

            def scores(n):
                br, tt, hp = n // 8, n // 4 % 2, n % 4
                b = open_bank(pe, "s", n)
                if n == 8:
                    for t in range(TT):
                        drained(pe, "mqT", t, 1), drained(pe, "mkT", t, 1)
                for hh in range(2):
                    if br == 0:
                        lhs = qT[hh * 64:(hh + 1) * 64, hp, tt * P:(tt + 1) * P]
                        rhs = kT[hh * 64:(hh + 1) * 64, hp, :]
                    else:
                        lhs, rhs = mqT[:, 2 * hp + hh, tt * P:(tt + 1) * P], mkT[:, 2 * hp + hh, :]
                    ins = pe.matmul(b[:, hh * 256:(hh + 1) * 256], lhs, rhs, start=True, stop=True)
                    if br == 0 and hh == 0:
                        ins.then_inc(head_scored, 1)
                        pe.wait_ge(head_scored, n + 1)
                ins.then_inc(full_f, 1)

            scores(0)
            scores(1)
            for n in range(16):
                br, tt, hp = n // 8, n // 4 % 2, n % 4
                pe.wait_ge(exps, n + 1)
                b = open_bank(pe, "pT", n)
                for cc in range(4):
                    ins = pe.transpose(b[:, cc * P:(cc + 1) * P], p_sb[:, n % 2, cc // 2, (cc % 2) * P:(cc % 2 + 1) * P], ident)
                ins.then_inc(full_f, 1)
                if n + 2 < 16:
                    scores(n + 2)
                drained(pe, "pT", n)
                o = open_bank(pe, "o", n // 4) if hp == 0 else bank("o", n // 4)
                vv = v_m if br else v_na
                for hh in range(2):
                    hd = 2 * hp + hh
                    for kc in range(2):
                        ins = pe.matmul(o[:, hd * 64:(hd + 1) * 64], pT[:, n % 2, 2 * hh + kc], vv[:, kc, hd * 64:(hd + 1) * 64], start=(kc == 0), stop=(kc == 1))
                ins.then_inc(pv, 1)
                if n % 4 == 2:
                    two_tiles(("gate", n // 4), [("gate", n // 4, t) for t in range(TT)], 2)
                if n in MOD_AFTER:
                    mod(MOD_AFTER[n])
            for a in range(4):
                drained(pe, "o", a)
                b = open_bank(pe, "oT", a)
                for cc in range(4):
                    ins = pe.transpose(b[:, cc * P:(cc + 1) * P], o_sb[:, a, cc * P:(cc + 1) * P], ident)
                ins.then_inc(full_f, 1)
            for br in range(2):
                for tt in range(TT):
                    drained(pe, "oT", 2 * br + tt)
                banks = [[open_bank(pe, "up", br, tt, half) for half in range(2)] for tt in range(TT)]
                for u in range(2):
                    arrived(pe, "up", br, u)
                    view = unit_at("up", br, u).rearrange("p (k n) -> p k n", k=2)
                    for tt in range(TT):
                        for half in range(2):
                            for i in range(2):
                                ins = pe.matmul(banks[tt][half][:], oT[:, 4 * br + 2 * u + i, tt * P:(tt + 1) * P], view[:, i, half * BANK:(half + 1) * BANK], start=(u == 0 and i == 0), stop=(u == 1 and i == 1))
                            if u == 1:
                                ins.then_inc(full_f, 1)
                    if u == 0:
                        ins.then_inc(pe_used, 1)
            turn_tile("mT", h, merged_s, 2)
            for tt in range(TT):
                for q in range(2):
                    drained(pe, "mT", tt, q)
            banks = [[open_bank(pe, "y", tt, half) for half in range(2)] for tt in range(TT)]
            for u in range(4):
                arrived(pe, "out", u)
                view = unit_at("out", u).rearrange("p (k n) -> p k n", k=2)
                for tt in range(TT):
                    for half in range(2):
                        for i in range(2):
                            ins = pe.matmul(banks[tt][half][:], hidden(tt, 2 * u + i), view[:, i, half * BANK:(half + 1) * BANK], start=(u == 0 and i == 0), stop=(u == 3 and i == 1))
                        if u == 3:
                            ins.then_inc(full_f, 1)
                if u < 3:
                    ins.then_inc(pe_used, 1)
            turn_tile("h2T", h, h2_made, 1)
            pe.wait_ge(router_in, 32)
            for tt in range(TT):
                for q in range(2):
                    drained(pe, "h2T", tt, q)
                b = open_bank(pe, "lg", tt)
                for k in range(KD):
                    ins = pe.matmul(b[:, 0:NE], hidden(tt, k), wr[:, k], start=(k == 0), stop=(k == KD - 1))
                ins.then_inc(full_f, 1)
            MASK, GATE = 10, 12
            for tt in range(TT):
                pe.wait_ge(mask_made, tt + 1)
                b = open_bank(pe, "pos", tt)
                if tt:
                    pe.matmul(b[:, 0:NE], ones, rt[:, MASK], start=True, stop=False)
                pe.matmul(b[:, 0:NE], tri, rt[:, MASK + tt], start=(tt == 0), stop=True).then_inc(full_f, 1)
            b = open_bank(pe, "cnt")
            for tt in range(TT):
                ins = pe.matmul(b[:, 0:NE], ones, rt[:, MASK + tt], start=(tt == 0), stop=(tt == 1))
            ins.then_inc(full_f, 1)
            for tt in range(TT):
                pe.wait_ge(gate_made, tt + 1)
                b = open_bank(pe, "gT", tt)
                pe.transpose(b[0:NE, 0:P], rt[:, GATE + tt], ident).then_inc(full_f, 1)
            pe.wait_ge(b2_in, 16)
            for tt in range(TT):
                drained(pe, "gT", tt)
                for half in range(2):
                    b = open_bank(pe, "b2", tt, half)
                    pe.matmul(b[:], gT[:, tt * P:(tt + 1) * P], b2sb[:, half * BANK:(half + 1) * BANK], start=True, stop=True).then_inc(full_f, 1)
            pe.wait_ge(out_act, front_drains["act"])
            pe.wait_ge(out_dve, front_drains["dve"])
            pe.wait_ge(xhi_made, 2)
            pe.wait_ge(xlo_made, 2)
            pe.wait_ge(tabs_made, 1)

            def free(count, r):
                by_act, n = count
                pe.wait_ge(drain_act if by_act else drain_dve, n + r * (NE if by_act else DVE_DRAINS))

            def gather_fill(q, target):
                for cc in range(4):
                    k = 4 * (q % 2) + cc
                    dst = target[:, cc * P:(cc + 1) * P]
                    for tt in range(TT):
                        src = xs_hi if q < 2 else xs_lo
                        ins = pe.matmul(dst, src[:, tt, k], sel_t[:, tt], start=(tt == 0), stop=(tt == 1 and q >= 2), skip_group_check=True)
                    if q < 2:
                        for tt in range(TT):
                            ins = pe.matmul(dst[:, HALF:P], xs_lo[:, tt, k], sela_t[:, tt, HALF:P], start=False, stop=(tt == 1), skip_group_check=True)
                ins.then_inc(gather_full, 1)

            def sweep(r):
                def flag(e):
                    if r:
                        return None
                    return pe.value_load(cnt_i[0:1, e:e + 1] if isinstance(e, int) else cnt_i[0:1, bass.ds(e, 1)], min_val=0, max_val=TT * P)

                def many(count, body):
                    if count is None:
                        body()
                    else:
                        with pe.If(count > half_cap):
                            body()

                def w1_unit(m_no, q, slot, k, par, count, lo_wait):
                    pe.wait_ge(hi_ready, r * UNITS + m_no + 1)
                    for n4 in range(4):
                        pe.matmul(ps[n4][:], t1[:, par, k], whi[:, q, n4 * BANK:(n4 + 1) * BANK], start=(k == 0), stop=False, skip_group_check=True)
                    wait_lo(pe, lo_wait, r)

                    def lo_tokens():
                        for n4 in range(4):
                            pe.matmul(ps[n4][:], t2[:, par, k], whi[:, q, n4 * BANK:(n4 + 1) * BANK], start=False, stop=False, skip_group_check=True)

                    many(count, lo_tokens)
                    for n4 in range(4):
                        ins = pe.matmul(ps[n4][:], t1[:, par, k], ring_lo[:, slot, n4 * BANK:(n4 + 1) * BANK], start=False, stop=(k == KD - 1), skip_group_check=True)
                    ins.then_inc(split_used, 1)

                def first_gather(e):
                    pe.wait_ge(sel_made, r * (NE + 1) + e + 1)
                    if r:
                        pe.wait_ge(drain_dve, DVE_DRAINS)
                    for q in range(4):
                        gather_fill(q, ps[4 * e + q])

                first_gather(0)
                pe.wait_ge(gather_used, r * 4 * NE + 4)
                count = flag(0)
                for m in range(8):
                    if m == 5:
                        first_gather(1)
                    w1_unit(m, m % SPLITS, (NF + m) % SLOTS, m, 0, count, lo_count_of_unit(m))

                def turn_shares(e, b):
                    pe.wait_ge(w_made, r * NE + e)
                    free(two_before(e, "w"), r)
                    for tt in range(TT):
                        ins = pe.transpose(ps[6 + bank_of(e, "w", b)][:, tt * P:(tt + 1) * P], wsel[:, tt], ident)
                    ins.then_inc(misc_full, 1)

                def combine(e, b):
                    pe.wait_ge(ys_made, r * NE + e)
                    free(drains(e, "w"), r)
                    for q in range(4):
                        kind = "c%d" % q
                        free(two_before(e, kind), r)
                        pe.matmul(ps[6 + bank_of(e, kind, b)][:], wT[:, (q // 2) * P:(q // 2 + 1) * P], ys[:, (q % 2) * BANK:(q % 2 + 1) * BANK],
                                  start=True, stop=True).then_inc(misc_full, 1)

                def step(e, b):
                    par = (e if isinstance(e, int) else b) % 2
                    count = flag(e)
                    following = None if last(e) else flag(e + 1)
                    if not first_step(e):
                        turn_shares(e, b)
                    pe.wait_ge(hs_act, r * NE + e + 1)
                    pe.wait_ge(hs_dve, r * NE + e + 1)
                    if not no_gather(e):
                        pe.wait_ge(sel_made, r * (NE + 1) + e + 3)
                        for q in range(4):
                            gather_fill(q, ps[q])
                    pe.wait_ge(fold_made, r * NE + e + 1)
                    if first_step(e):
                        pe.wait_ge(gather_used, r * 4 * NE + 8)
                    turned = hs[:].rearrange("s (p k g) -> s g k p", k=KD, g=2)
                    for f in range(4):
                        kind = "f%d" % f
                        if two_before(e, kind) is not None:
                            free(two_before(e, kind), r)
                        dst = ps[6 + bank_of(e, kind, b)]
                        for g in range(2):
                            for kk in range(2):
                                cc = 2 * g + kk
                                ins = pe.matmul(dst[:, cc * P:(cc + 1) * P], turned[:, g, 2 * f + kk, :], fmat[:], start=True, stop=True)
                        ins.then_inc(misc_full, 1)
                    if not first_step(e):
                        combine(e, b)
                    if not last(e):
                        pe.wait_ge(gather_used, r * 4 * NE + (4 * NE if no_gather(e) else 4 * (e + 3)))
                        for j in range(8):
                            w1_unit(unit_no(e, j), split_slot(e, j), ring_slot(e, b, j, NF), j, 1 - par, following, lo_count(e, j))
                    pe.wait_ge(u_ready, r * NE + e + 1)
                    for j in range(8, 12):
                        q = split_slot(e, j)
                        hi_v = whi[:, q].rearrange("p (k n) -> p k n", k=2)
                        lo_v = ring_lo[:, ring_slot(e, b, j, NF)].rearrange("p (k n) -> p k n", k=2)
                        pe.wait_ge(hi_ready, r * UNITS + unit_no(e, j) + 1)

                        def products(u, w, starts, stops):
                            for i in range(2):
                                kk = 2 * (j - 8) + i
                                for half in range(2):
                                    ins = pe.matmul(ps[4 + half][:], u[:, kk], w[:, i, half * BANK:(half + 1) * BANK],
                                                    start=(starts and kk == 0), stop=(stops and kk == KD - 1), skip_group_check=True)
                            return ins

                        products(u1, hi_v, True, False)
                        wait_lo(pe, lo_count(e, j), r)

                        def lo_slots():
                            products(u2, hi_v, False, False)

                        many(count, lo_slots)
                        products(u1, lo_v, False, True).then_inc(split_used, 1)

                over_experts(pe, step)
                turn_shares(NE, 0)
                combine(NE, 0)

            two_sweeps(pe, sweep)


_INS = ["x", "c", "w_ada", "b_ada", "g_attn_pre", "g_attn_post", "w_in", "b_gate", "na_rpb", "q_norm_g", "kv_norm_g",
        "w_uq", "w_ukv", "w_na_up", "w_mla_up", "w_out", "g_ffn_pre", "g_ffn_post", "w_router", "b_router",
        "w1", "b1", "w2", "b2"]


def constants():
    import numpy as np

    p, j = np.arange(P)[:, None], np.arange(P)[None, :]
    con = np.zeros((P, C_WIDTH), np.float32)
    con[:, C_ID:C_ID + P] = p == j
    con[:, C_TRI:C_TRI + P] = p < j
    con[:, C_ONE:C_ONE + P] = 1
    con[:, C_J:C_J + P] = j
    con[:, C_JM:C_JM + P] = j % HALF
    con[:, C_OFF:C_OFF + P] = abs(p - j) == HALF
    con[:, C_FLIP:C_FLIP + P] = (p // GRID == j // GRID) & (p % GRID == GRID - 1 - j % GRID)
    qc, kc = np.arange(P)[:, None] % GRID, np.arange(GRID)[None, :]
    first = np.clip(qc - 8, 0, GRID - 16)
    con[:, C_MASK:C_MASK + GRID] = np.where((kc >= first) & (kc < first + 16), 0, -1e30)
    nf = ROPE // 4
    inv = np.float32(100.0) ** (-np.arange(nf, dtype=np.float32) / np.float32(nf))
    for tt in range(TT):
        t = tt * P + np.arange(P)
        for a, position in enumerate((t // GRID, t % GRID)):
            angle = position.astype(np.float32)[:, None] * inv
            o = 16 * tt + 8 * a
            con[:, C_COS + o:C_COS + o + 8] = np.cos(angle)
            con[:, C_SIN + o:C_SIN + o + 8] = np.sin(angle)
    return con


def kernel(**inputs):
    import numpy as np
    import concourse.bacc as bacc
    from concourse.bass_utils import run_bass_kernel_spmd

    nc = bacc.Bacc("TRN2", target_bir_lowering=False, num_devices=1)
    arrays, args = {}, []
    for name in _INS:
        a = np.ascontiguousarray(inputs[name])
        arrays[f"in_{name}"] = a
        args.append(nc.dram_tensor(f"in_{name}", a.shape, mybir.dt.from_np(a.dtype), kind="ExternalInput").ap())
    arrays["in_consts"] = constants()
    args.append(nc.dram_tensor("in_consts", (P, C_WIDTH), F32, kind="ExternalInput").ap())
    args.append(nc.dram_tensor("out_x", (1, TT * P, D), F32, kind="ExternalOutput").ap())
    build(nc, *args)
    r = run_bass_kernel_spmd(nc, [arrays], core_ids=[0])
    return r.results[0]["out_x"]
```
